# Optimizing a Trainium2 kernel written in Bass

```python
import math
import jax, jax.numpy as jnp
from jax import lax
import numpy as np

D_MODEL = 1024
BATCH = 1
SEQ = 512
DEPTH = 1
DEC_BATCH = 8
DEC_SEQ = 8
PAST_LEN = 4096
PAGE_SIZE = 128

D_MIX = D_MODEL
D_POOL = D_MIX // 2
D_CONV = D_MIX - D_POOL
POOL_WINDOWS = (2, 4, 8, 16)
N_POOL_GROUPS = len(POOL_WINDOWS)
POOL_GROUP = D_POOL // N_POOL_GROUPS
POOL_STATE = max(POOL_WINDOWS) - 1
CONV_HEADS = 8
CONV_HEAD_DIM = D_CONV // CONV_HEADS
CONV_W = 3
D_IN = D_POOL + 3 * D_CONV
N_EXPERT_GROUPS = 4
EXPERTS_PER_GROUP = 8
N_EXPERTS = N_EXPERT_GROUPS * EXPERTS_PER_GROUP
TOP_K_IN_GROUP = 2
D_EXPERT = D_MODEL // 2
DEEPNORM_ALPHA = (2.0 * DEPTH) ** 0.25
DEEPNORM_BETA = (8.0 * DEPTH) ** -0.25
LN_EPS = 1e-5

kernel_name = "hymba_pool_shortconv_hiermoe_step"

def _layer_norm(x, g, b):
    xf = x.astype(jnp.float32)
    mu = jnp.mean(xf, axis=-1, keepdims=True)
    var = jnp.mean(jnp.square(xf - mu), axis=-1, keepdims=True)
    y = (xf - mu) * lax.rsqrt(var + LN_EPS)
    return (y * g.astype(jnp.float32) + b.astype(jnp.float32)).astype(x.dtype)

def _mixer(x, pool_prev, conv_prev, start_pos, w_in, w_pool_map, pool_scale, conv_w, w_out):
    bsz, T, _ = x.shape
    h = jnp.einsum('btd,de->bte', x, w_in)
    v = h[..., :D_POOL]
    gate_b = h[..., D_POOL:D_POOL + D_CONV]
    gate_c = h[..., D_POOL + D_CONV:D_POOL + 2 * D_CONV]
    xc = h[..., D_POOL + 2 * D_CONV:]

    v_ext = jnp.concatenate([pool_prev.astype(v.dtype), v], axis=1)
    cs = jnp.cumsum(v_ext.astype(jnp.float32), axis=1)
    cs0 = jnp.concatenate([jnp.zeros((bsz, 1, D_POOL), jnp.float32), cs], axis=1)
    pos = start_pos + jnp.arange(T)
    pool_outs = []
    for g, w in enumerate(POOL_WINDOWS):
        sl = slice(g * POOL_GROUP, (g + 1) * POOL_GROUP)
        hi = cs0[:, POOL_STATE + 1:POOL_STATE + 1 + T, sl]
        lo = cs0[:, POOL_STATE + 1 - w:POOL_STATE + 1 - w + T, sl]
        cnt = jnp.minimum(w, pos + 1).astype(jnp.float32)[None, :, None]
        pooled = (hi - lo) / cnt - v[:, :, sl].astype(jnp.float32)
        pool_outs.append(jnp.einsum('btc,ce->bte', pooled.astype(x.dtype), w_pool_map[g]))
    pool_out = jnp.concatenate(pool_outs, axis=-1) * pool_scale
    new_pool = v_ext[:, -POOL_STATE:]

    u = gate_c * xc
    u_ext = jnp.concatenate([conv_prev.astype(u.dtype), u], axis=1)
    conv = sum(conv_w[k] * u_ext[:, k:k + T] for k in range(CONV_W))
    conv_out = gate_b * conv
    new_conv = u_ext[:, -(CONV_W - 1):]

    y = jnp.einsum('bte,ed->btd', jnp.concatenate([pool_out, conv_out], axis=-1), w_out)
    return y, new_pool, new_conv

def _hier_moe(x, w_group, b_group, w_expert, b_expert, w1, w3, w2):
    bsz, T, d = x.shape
    xf = x.reshape(bsz * T, d)
    n = xf.shape[0]
    g_logits = (xf @ w_group + b_group).astype(jnp.float32)
    g_prob = jax.nn.softmax(g_logits, axis=-1)
    g_top, g_idx = lax.top_k(g_prob, 1)
    e_logits = (xf @ w_expert + b_expert).astype(jnp.float32)
    e_logits = e_logits.reshape(n, N_EXPERT_GROUPS, EXPERTS_PER_GROUP)
    e_in_group = jnp.take_along_axis(e_logits, g_idx[:, :, None], axis=1)[:, 0]
    e_prob = jax.nn.softmax(e_in_group, axis=-1)
    e_top, e_idx = lax.top_k(e_prob, TOP_K_IN_GROUP)
    e_top = e_top / jnp.sum(e_top, axis=-1, keepdims=True)
    gate = g_top * e_top
    global_idx = g_idx * EXPERTS_PER_GROUP + e_idx
    combine = jnp.sum(jax.nn.one_hot(global_idx, N_EXPERTS, dtype=jnp.float32)
                      * gate[..., None], axis=1)
    combine = combine.astype(x.dtype)
    acc = jnp.zeros((n, d), x.dtype)
    for e in range(N_EXPERTS):
        hdn = jax.nn.silu(xf @ w1[e]) * (xf @ w3[e])
        acc = acc + combine[:, e:e + 1] * (hdn @ w2[e])
    return acc.reshape(bsz, T, d)

def _layer(x, pool_prev, conv_prev, start_pos, w_in, w_pool_map, pool_scale, conv_w, w_out,
           ln1_g, ln1_b, w_group, b_group, w_expert, b_expert, w1, w3, w2, ln2_g, ln2_b):
    m, new_pool, new_conv = _mixer(x, pool_prev, conv_prev, start_pos,
                                   w_in, w_pool_map, pool_scale, conv_w, w_out)
    x = _layer_norm(DEEPNORM_ALPHA * x + m, ln1_g, ln1_b)
    f = _hier_moe(x, w_group, b_group, w_expert, b_expert, w1, w3, w2)
    x = _layer_norm(DEEPNORM_ALPHA * x + f, ln2_g, ln2_b)
    return x, new_pool, new_conv

def setup_inputs(seed: int = 0) -> dict:
    key = jax.random.key(seed)
    ks = jax.random.split(key, 20)
    f32 = jnp.float32
    nrm = lambda k, shape, s: jax.random.normal(k, shape, f32) * s
    return {
        "x_prompt": nrm(ks[0], (BATCH, SEQ, D_MODEL), 1.0),
        "x_sample": nrm(ks[1], (DEC_BATCH, DEC_SEQ, D_MODEL), 1.0),
        "state_pool": nrm(ks[2], (DEC_BATCH, POOL_STATE, D_POOL), 1.0),
        "state_conv": nrm(ks[3], (DEC_BATCH, CONV_W - 1, D_CONV), 1.0),
        "w_in": nrm(ks[4], (D_MODEL, D_IN), D_MODEL ** -0.5),
        "w_pool_map": nrm(ks[5], (N_POOL_GROUPS, POOL_GROUP, POOL_GROUP), POOL_GROUP ** -0.5),
        "pool_scale": 1.0 + nrm(ks[6], (D_POOL,), 0.02),
        "conv_w": nrm(ks[7], (CONV_W, D_CONV), CONV_W ** -0.5),
        "w_out": nrm(ks[8], (D_MIX, D_MODEL), D_MIX ** -0.5 * DEEPNORM_BETA),
        "ln1_g": 1.0 + nrm(ks[9], (D_MODEL,), 0.02),
        "ln1_b": nrm(ks[10], (D_MODEL,), 0.02),
        "w_group": nrm(ks[11], (D_MODEL, N_EXPERT_GROUPS), D_MODEL ** -0.5),
        "b_group": nrm(ks[12], (N_EXPERT_GROUPS,), 0.01),
        "w_expert": nrm(ks[13], (D_MODEL, N_EXPERTS), D_MODEL ** -0.5),
        "b_expert": nrm(ks[14], (N_EXPERTS,), 0.01),
        "w1": nrm(ks[15], (N_EXPERTS, D_MODEL, D_EXPERT), D_MODEL ** -0.5),
        "w3": nrm(ks[16], (N_EXPERTS, D_MODEL, D_EXPERT), D_MODEL ** -0.5),
        "w2": nrm(ks[17], (N_EXPERTS, D_EXPERT, D_MODEL), D_EXPERT ** -0.5 * DEEPNORM_BETA),
        "ln2_g": 1.0 + nrm(ks[18], (D_MODEL,), 0.02),
        "ln2_b": nrm(ks[19], (D_MODEL,), 0.02),
    }

def reference(x_prompt, x_sample, state_pool, state_conv, w_in, w_pool_map, pool_scale, conv_w,
              w_out, ln1_g, ln1_b, w_group, b_group, w_expert, b_expert, w1, w3, w2,
              ln2_g, ln2_b):
    weights = (w_in, w_pool_map, pool_scale, conv_w, w_out, ln1_g, ln1_b,
               w_group, b_group, w_expert, b_expert, w1, w3, w2, ln2_g, ln2_b)
    yp = x_prompt
    bp = x_prompt.shape[0]
    pool_p = jnp.zeros((bp, POOL_STATE, D_POOL), x_prompt.dtype)
    conv_p = jnp.zeros((bp, CONV_W - 1, D_CONV), x_prompt.dtype)
    ys = x_sample
    pool_s = state_pool
    conv_s = state_conv
    for _ in range(DEPTH):
        yp, new_pool_prompt, new_conv_prompt = _layer(yp, pool_p, conv_p, 0, *weights)
        ys, new_pool_sample, new_conv_sample = _layer(ys, pool_s, conv_s, PAST_LEN, *weights)
    return (yp, ys, new_pool_prompt, new_conv_prompt, new_pool_sample, new_conv_sample)


_drawn_inputs = setup_inputs


def setup_inputs(seed=0):
    import zlib

    import numpy as np

    out = dict(_drawn_inputs(seed))
    spreads = {}
    factors = {'pool_scale': 11.355, 'b_group': 8.0, 'b_expert': 22.51, 'ln2_g': 8.368, 'ln2_b': 8.213}
    for name, (base, spread) in spreads.items():
        noise = np.random.default_rng([zlib.crc32(name.encode()), seed]).standard_normal(out[name].shape)
        drawn = base * np.exp(spread * noise) if base else spread * noise
        out[name] = __import__('jax').numpy.asarray(drawn.astype(out[name].dtype))
    for name, factor in factors.items():
        out[name] = (out[name] * factor).astype(out[name].dtype)
    return out
```

```python
from contextlib import ExitStack

import concourse.bass as bass
from concourse import mybir

F32 = mybir.dt.float32
BF16 = mybir.dt.bfloat16
I32 = mybir.dt.int32
ALU = mybir.AluOpType
ACT = mybir.ActivationFunctionType
AX = mybir.AxisListType

P = 128
D = 1024
KD = D // P
SEQ = 512
NB, NS = 8, 8
T = SEQ + NB * NS
HALF = T // 2
NT = 5
ROWS = [P, P, P, P, NB * NS]
DP = 512
NG = DP // P
HIST, CHIST = 15, 2
PV = HIST + SEQ
VEXT = PV + NB * (HIST + NS)
PU = CHIST + SEQ
UEXT = PU + NB * (CHIST + NS)
VTAIL = HIST * (1 + NB)
UTAIL = CHIST * (1 + NB)
EG, EPG = 4, 8
E = EG * EPG
NR = EG + E
F = 512
KF = F // P
SLOTS = 80
XTILES = (2 * T) // SLOTS
TILES = E + XTILES
NQ = (T - 1) // SLOTS
ALPHA = 2.0 ** 0.25
EPS = 1e-5
RING = 3
BLK = KD * F
PAD = 8192


def build(nc, x_prompt, x_sample, state_pool, state_conv, w_in, w_pool_map, pool_scale, conv_w, w_out,
          ln1_g, ln1_b, w_group, b_group, w_expert, b_expert, w1, w3, w2, ln2_g, ln2_b,
          y_prompt, y_sample, pool_prompt, conv_prompt, pool_sample, conv_sample):
    ctx = ExitStack()
    with ctx:
        def sb(name, shape, dt=F32):
            return ctx.enter_context(nc.sbuf_tensor(name, shape, dt))

        def sem(name):
            return ctx.enter_context(nc.semaphore(name))

        x1_dram = nc.dram_tensor("x1_rows", (T, D), F32).ap()
        y_dram = nc.dram_tensor("expert_rows", (2 * T, D), F32).ap()

        x_tok = sb("x_tok", [P, NT, D])
        blocks = sb("blocks", [P, 9, BLK])
        io = sb("io", [P, 6, D])
        xeT = sb("xeT", [P, KD, SLOTS])
        hT = sb("hT", [P, KF, SLOTS])
        silu = sb("silu", [P, 2, SLOTS])
        w_router = sb("w_router", [P, KD, NR])
        b_router = sb("b_router", [P, NR])
        ln1 = sb("ln1", [P, 2, D])
        ident = sb("ident", [P, P])
        before = sb("before", [P, P], BF16)
        ones = sb("ones", [P, P], BF16)
        iota = sb("iota", [P, SLOTS])
        rev = sb("rev", [P, EPG])
        edges = sb("edges", [P, NQ])
        tokval = sb("tokval", [P, NT, 3])
        chan = sb("chan", [P, NG, 4])
        w_map = sb("w_map", [P, NG, P])
        logits = sb("logits", [P, NT, NR])
        stats = sb("stats", [P, 2, 6])
        mv = sb("mv", [P, 2])
        rstd = sb("rstd", [P, 4])
        std = sb("std", [P, 1])
        eps = sb("eps", [P, 1])
        gates = sb("gates", [P, NT, 2])
        slot_rows = sb("slot_rows", [P, 2, TILES], I32)
        gather_idx = sb("gather_idx", [P, RING], I32)
        scatter_idx = sb("scatter_idx", [P, RING], I32)
        extra = sb("extra", [1, XTILES + 1], I32)

        w1_slot = [blocks[:, b, :].rearrange("p (k f) -> p k f", k=KD) for b in (0, 3, 7)]
        w3_slot = [blocks[:, b, :].rearrange("p (k f) -> p k f", k=KD) for b in (1, 4, 8)]
        w2_slot = [blocks[:, b, :].rearrange("p (k d) -> p k d", k=KF) for b in (2, 5, 6)]
        xe = [io[:, u, :] for u in range(RING)]
        ye = [io[:, RING + u, :] for u in range(RING)]

        win_a = blocks[:, 7, :].rearrange("p (k c) -> p k c", k=KD)
        win_b = blocks[:, 8, :].rearrange("p (k c) -> p k c", k=KD)
        area = blocks[:, 5:7, :].rearrange("p a b -> p (a b)")
        xT = area[:, 0:KD * T].rearrange("p (k t) -> p k t", k=KD)
        at = KD * T
        vext = [area[:, at + i * VEXT:at + (i + 1) * VEXT] for i in range(2)]
        wsum = [area[:, at + (2 + i) * VEXT:at + (3 + i) * VEXT] for i in range(2)]
        pooled = area[:, at + 4 * VEXT:at + 4 * VEXT + T]
        io_flat = io[:, :, :].rearrange("p a b -> p (a b)")
        mixT = io_flat[:, 0:2 * NG * T].rearrange("p (j t) -> p j t", j=2 * NG)
        at = 2 * NG * T
        x1T = io_flat[:, at:at + D].rearrange("p (k t) -> p k t", k=KD)
        vtail = io_flat[:, at:at + NG * VTAIL].rearrange("p (j t) -> p j t", j=NG)
        at += NG * VTAIL
        poolT = io_flat[:, at:at + NG * NB * HIST].rearrange("p (j t) -> p j t", j=NG)
        at += NG * NB * HIST
        convT = io_flat[:, at:at + NG * NB * CHIST].rearrange("p (j t) -> p j t", j=NG)
        at += NG * NB * CHIST
        utail = io_flat[:, at:at + NG * UTAIL].rearrange("p (j t) -> p j t", j=NG)
        xeT_flat = xeT[:, :, :].rearrange("p k t -> p (k t)")
        pool_rows = ln1[:, 0, 0:DP]
        conv_rows = ln1[:, 0, DP:2 * DP]
        chan_rows = ln1[:, 1, 0:DP]
        counts = xeT_flat[:, 0:HIST]

        def router_memory():
            areas = [[3 * D, 2 * NG * T], [2 * NG * T + D, 6 * D]]

            def take(*shape):
                n = 1
                for s in shape:
                    n *= s
                a = next(a for a in areas if a[0] + n <= a[1])
                a[0] += n
                v = io_flat[:, a[0] - n:a[0]]
                names = ["a", "b", "c", "d"][:len(shape)]
                if len(shape) > 1:
                    v = v.rearrange(f"p ({' '.join(names)}) -> p {' '.join(names)}",
                                    **dict(zip(names[1:], shape[1:])))
                return v
            return take

        take = router_memory()
        picked = take(NT, 2, E)
        product = take(NT, 2, E)
        mask = take(NT, E // 2).bitcast(BF16)
        in_group = take(NT, E)
        past_cnt = take(E, NQ)
        past_pos = take(NT * 2, NQ)
        g_hot, g_tmp, g_exp = take(NT, EG), take(NT, EG), take(NT, EG)
        e_val, e_tmp = take(NT, EPG), take(NT, EPG)
        e_hot = take(NT, 2, EPG)
        top = take(4, NT)
        best = take(NT)
        lift = take(NT)
        cnt, further, upto, first = take(E), take(E), take(E), take(E)
        pos, quot, base, expert, tile_no, col = [take(NT * 2) for _ in range(6)]
        over = io_flat[:, 2300:2300 + XTILES * E].rearrange("p (a e) -> p a e", a=XTILES)
        over_n = take(XTILES)
        hot_col = io_flat[:, 0:10 * SLOTS].rearrange("p (a c) -> p a c", a=10)
        hot_tile = io_flat[:, 800:800 + 10 * TILES].rearrange("p (a c) -> p a c", a=10)
        slot_val = io_flat[:, 1300:1300 + 20 * TILES].rearrange("p (a b c) -> p a b c", a=10, b=2)

        head = blocks[:, 0:3, :].rearrange("p a b -> p (a b)")
        y_pair = head[:, 0:NT * 2 * D].rearrange("p (j k d) -> p j k d", j=NT, k=2)
        ln2 = head[:, NT * 2 * D:NT * 2 * D + 2 * D].rearrange("p (a d) -> p a d", a=2)

        ps = ctx.enter_context(nc.psum_tensor("ps", [P, 8, 512], F32))

        x_loaded = [sem(f"x_loaded{j}") for j in range(NT)]
        win_loaded = [sem(f"win_loaded{c}") for c in range(4)]
        wout_loaded = [sem(f"wout_loaded{h}") for h in range(2)]
        rows_loaded = sem("rows_loaded")
        router_loaded = sem("router_loaded")
        ln1_loaded = sem("ln1_loaded")
        consts_made = sem("consts_made")
        zeros_made = sem("zeros_made")
        x_turned = sem("x_turned")
        xT_act, xT_dve = sem("xT_act"), sem("xT_dve")
        rows_turned = sem("rows_turned")
        rows_kept = sem("rows_kept")
        in_done = sem("in_done")
        in_act, in_dve = sem("in_act"), sem("in_dve")
        pooled_ready = sem("pooled_ready")
        map_done, map_kept = sem("map_done"), sem("map_kept")
        vtail_kept, utail_kept = sem("vtail_kept"), sem("utail_kept")
        tail_turned, tail_kept = sem("tail_turned"), sem("tail_kept")
        tail_stored = sem("tail_stored")
        out_done, out_kept = sem("out_done"), sem("out_kept")
        x1_scaled, x1_ready, x1_stored = sem("x1_scaled"), sem("x1_ready"), sem("x1_stored")
        var_ready, std_ready = sem("var_ready"), sem("std_ready")
        x1_turned = sem("x1_turned")
        x1T_act, x1T_dve = sem("x1T_act"), sem("x1T_dve")
        logits_done, logits_kept = sem("logits_done"), sem("logits_kept")
        diff_ready, exp_ready = sem("diff_ready"), sem("exp_ready")
        mask_ready = sem("mask_ready")
        pos_done = sem("pos_done")
        hot_ready = sem("hot_ready")
        table_done, table_ready = sem("table_done"), sem("table_ready")
        extra_ready = sem("extra_ready")
        w1_loaded = [sem(f"w1_loaded{u}") for u in range(RING)]
        w3_loaded = [sem(f"w3_loaded{u}") for u in range(RING)]
        w2_loaded = [sem(f"w2_loaded{u}") for u in range(RING)]
        gathered = [sem(f"gathered{u}") for u in range(RING)]
        scattered = [sem(f"scattered{u}") for u in range(RING)]
        gather_col, scatter_col = sem("gather_col"), sem("scatter_col")
        issued = sem("issued")
        xe_turned = sem("xe_turned")
        xeT_act, xeT_dve = sem("xeT_act"), sem("xeT_dve")
        h_done, silu_ready, h_ready = sem("h_done"), sem("silu_ready"), sem("h_ready")
        ylo_done, yhi_done = sem("ylo_done"), sem("yhi_done")
        ylo_kept, yhi_kept = sem("ylo_kept"), sem("yhi_kept")
        ln2_loaded = sem("ln2_loaded")
        y_loaded = [sem(f"y_loaded{j}") for j in range(NT)]
        stats_ready, centred, gained = sem("stats_ready"), sem("centred"), sem("gained")
        out_ready, out_stored = sem("out_ready"), sem("out_stored")
        step = sem("step")

        block = ctx.enter_context(nc.Block())

        def wait(eng, semaphore, value):
            if not (isinstance(value, int) and value == 0):
                eng.wait_ge(semaphore, value)

        def token_rows(tensor_prompt, tensor_sample, j):
            if j < NT - 1:
                return tensor_prompt[0, j * P:(j + 1) * P, :]
            return tensor_sample.rearrange("b s d -> (b s) d")

        @block.sync
        def _(sp):
            win = w_in.rearrange("(p k) c -> p k c", k=KD)
            wout = w_out.rearrange("(j p) d -> p j d", p=P)

            for j in range(NT):
                sp.dma_start(x_tok[0:ROWS[j], j, :], token_rows(x_prompt, x_sample, j)).then_inc(x_loaded[j], 16)
            sp.dma_start(win_a, win[:, :, 0:DP]).then_inc(win_loaded[0], 16)
            sp.dma_start(pool_rows[0:NB * HIST, :], state_pool.rearrange("b h c -> (b h) c")).then_inc(rows_loaded, 16)
            sp.dma_start(conv_rows[0:NB * CHIST, :], state_conv.rearrange("b h c -> (b h) c")).then_inc(rows_loaded, 16)
            sp.dma_start(chan_rows[0:3, :], conv_w).then_inc(rows_loaded, 16)
            sp.dma_start(chan_rows[3:4, :], pool_scale.rearrange("(a c) -> a c", a=1)).then_inc(rows_loaded, 16)
            sp.dma_start(w_map[:, :, :], w_pool_map.rearrange("g c e -> c g e")).then_inc(rows_loaded, 16)
            sp.dma_start(win_b, win[:, :, 2 * DP:3 * DP]).then_inc(win_loaded[1], 16)
            sp.dma_start(w_router[:, :, 0:EG], w_group.rearrange("(p k) c -> p k c", k=KD)).then_inc(router_loaded, 16)
            sp.dma_start(w_router[:, :, EG:NR], w_expert.rearrange("(p k) c -> p k c", k=KD)).then_inc(router_loaded, 16)
            sp.dma_start(b_router[:, 0:EG], b_group.partition_broadcast(P)).then_inc(router_loaded, 16)
            sp.dma_start(b_router[:, EG:NR], b_expert.partition_broadcast(P)).then_inc(router_loaded, 16)
            sp.wait_ge(rows_kept, 2)
            sp.dma_start(ln1[:, 0, :], ln1_g.partition_broadcast(P)).then_inc(ln1_loaded, 16)
            sp.dma_start(ln1[:, 1, :], ln1_b.partition_broadcast(P)).then_inc(ln1_loaded, 16)

            def load_w1(u, e):
                sp.dma_start(w1_slot[u], expert_matrix(w1, e, KD)).then_inc(w1_loaded[u], 16)

            def load_w3(u, e):
                sp.dma_start(w3_slot[u], expert_matrix(w3, e, KD)).then_inc(w3_loaded[u], 16)

            def load_w2(u, e):
                sp.dma_start(w2_slot[u], expert_w2(e)).then_inc(w2_loaded[u], 16)

            def expert_matrix(w, e, k):
                if isinstance(e, int):
                    return w[e].rearrange("(p k) f -> p k f", k=k)
                return w[bass.DynSlice(e, 1)].rearrange("e (p k) f -> p (e k) f", k=k)

            def expert_w2(e):
                if isinstance(e, int):
                    return w2[e].rearrange("(k p) d -> p k d", p=P)
                return w2[bass.DynSlice(e, 1)].rearrange("e (k p) d -> p (e k) d", p=P)

            load_w1(0, 0)
            load_w3(0, 0)
            load_w2(0, 0)
            sp.wait_ge(in_done, 4)
            sp.dma_start(win_a, win[:, :, 3 * DP:4 * DP]).then_inc(win_loaded[2], 16)
            load_w1(1, 1)
            load_w3(1, 1)
            sp.wait_ge(in_done, 8)
            sp.dma_start(win_b, win[:, :, DP:2 * DP]).then_inc(win_loaded[3], 16)
            sp.wait_ge(in_done, 12)
            sp.dma_start(win_a, wout[:, :, 0:512]).then_inc(wout_loaded[0], 16)
            sp.wait_ge(in_done, 16)
            sp.dma_start(win_b, wout[:, :, 512:D]).then_inc(wout_loaded[1], 16)
            sp.wait_ge(in_dve, 8)
            sp.wait_ge(utail_kept, NG)
            sp.wait_ge(tail_stored, 64)
            load_w2(1, 1)
            load_w2(2, 2)
            sp.wait_ge(out_done, NT)
            load_w1(2, 2)
            sp.wait_ge(out_done, 2 * NT)
            load_w3(2, 2)

            def load_tile(u, seq, e):
                sp.wait_ge(h_done, (seq - 2) * KF)
                load_w1(u, e)
                load_w3(u, e)
                sp.wait_ge(yhi_done, seq - 2)
                load_w2(u, e)

            with sp.Fori(1, E // RING) as n:
                for u in range(RING):
                    load_tile(u, n * RING + u, n * RING + u)
            for e in range(E // RING * RING, E):
                load_tile(e % RING, e, e)

            sp.wait_ge(extra_ready, 1)
            n_extra = sp.value_load(extra[0:1, XTILES:XTILES + 1], min_val=0, max_val=XTILES)
            with sp.If(n_extra > 0):
                with sp.Fori(0, n_extra) as v:
                    e = sp.value_load(extra[0:1, bass.DynSlice(v, 1)], min_val=0, max_val=E - 1)
                    sp.wait_ge(yhi_done, E + v)
                    load_w1(2, e)
                    load_w3(2, e)
                    load_w2(2, e)

            sp.wait_ge(yhi_done, E - 1)
            sp.dma_start(ln2[:, 0, :], ln2_g.partition_broadcast(P)).then_inc(ln2_loaded, 16)
            sp.dma_start(ln2[:, 1, :], ln2_b.partition_broadcast(P)).then_inc(ln2_loaded, 16)
            sp.wait_ge(scattered[0], 16 * 11)
            sp.wait_ge(scattered[1], 16 * 11)
            sp.wait_ge(scattered[2], n_extra * 16 + 160)
            y_rows = y_dram.rearrange("(t k) d -> t k d", k=2)
            for j in range(NT):
                sp.dma_start(y_pair[0:ROWS[j], j], y_rows[j * P:j * P + ROWS[j]]).then_inc(y_loaded[j], 16)
            for j in range(NT):
                sp.wait_ge(out_ready, j + 1)
                sp.dma_start(token_rows(y_prompt, y_sample, j), y_pair[0:ROWS[j], j, 0, :]).then_inc(out_stored, 16)
            sp.wait_ge(out_stored, 16 * NT)

        @block.tensor
        def _(pe):
            turn_banks = [4, 5, 0, 1, 2, 3]
            x_view = x_tok[:, :, :].rearrange("p j (q k) -> p j k q", k=KD)

            pe.wait_ge(consts_made, 1)
            for j in range(NT):
                r = ROWS[j]
                pe.wait_ge(x_loaded[j], 16)
                for h in range(2):
                    if j >= 3:
                        pe.wait_ge(xT_dve if h else xT_act, j - 2)
                    b = turn_banks[(2 * j + h) % 6]
                    for i in range(4):
                        mm = pe.transpose(ps[:, b, i * r:(i + 1) * r], x_view[0:r, j, 4 * h + i, :], ident[0:r, 0:r])
                    mm.then_inc(x_turned, 1)

            pe.wait_ge(rows_loaded, 80)
            for g in range(NG):
                mm = pe.transpose(ps[:, 6, g * 120:(g + 1) * 120], pool_rows[0:120, g * P:(g + 1) * P],
                                  ident[0:120, 0:120])
            mm.then_inc(rows_turned, 1)
            for g in range(NG):
                pe.transpose(ps[:, 7, g * 4:(g + 1) * 4], chan_rows[0:4, g * P:(g + 1) * P], ident[0:4, 0:4])
                mm = pe.transpose(ps[:, 7, 16 + g * 16:32 + g * 16], conv_rows[0:16, g * P:(g + 1) * P],
                                  ident[0:16, 0:16])
            mm.then_inc(rows_turned, 1)

            def project(c):
                part, g = c // NG, c % NG
                if g == 0:
                    pe.wait_ge(win_loaded[part], 16)
                if c in (2, 3) or 4 <= c < 10:
                    pe.wait_ge(in_act, c - 1)
                elif c >= 10:
                    pe.wait_ge(in_dve, c - 9)
                w = (win_a, win_b)[part % 2]
                for h in range(2):
                    for k in range(KD):
                        mm = pe.matmul(ps[:, 2 * (c % 2) + h, 0:HALF], w[:, k, g * P:(g + 1) * P],
                                       xT[:, k, h * HALF:(h + 1) * HALF], start=(k == 0), stop=(k == KD - 1))
                mm.then_inc(in_done, 1)

            def pool_map(g):
                pe.wait_ge(pooled_ready, g + 1)
                if g:
                    pe.wait_ge(map_kept, g)
                else:
                    pe.wait_ge(rows_kept, 2)
                for h in range(2):
                    mm = pe.matmul(ps[:, 6 + h, 0:HALF], w_map[:, g, :], pooled[:, h * HALF:(h + 1) * HALF],
                                   start=True, stop=True)
                mm.then_inc(map_done, 1)

            def turn_tail(tail, n):
                for g in range(NG):
                    pe.transpose(ps[0:n, 4, g * P:(g + 1) * P], tail[:, g, 0:n], ident[:, :])
                    mm = pe.transpose(ps[0:NB * n, 5, g * P:(g + 1) * P], tail[:, g, n:n + NB * n], ident[:, :])
                mm.then_inc(tail_turned, 1)

            pe.wait_ge(xT_act, NT)
            pe.wait_ge(xT_dve, NT)
            project(0)
            project(1)
            pool_map(0)
            project(2)
            pool_map(1)
            project(3)
            pool_map(2)
            project(4)
            pool_map(3)
            project(5)
            pe.wait_ge(vtail_kept, NG)
            turn_tail(vtail, HIST)
            for c in range(6, 13):
                project(c)
            pe.wait_ge(utail_kept, NG)
            pe.wait_ge(tail_kept, 1)
            turn_tail(utail, CHIST)
            for c in range(13, 16):
                project(c)

            def out_project(h, j):
                o = h * NT + j
                r = ROWS[j]
                if o >= 4:
                    pe.wait_ge(out_kept, o - 3)
                w = (win_a, win_b)[h]
                for k in range(KD):
                    mm = pe.matmul(ps[0:r, o % 4, :], mixT[:, k, j * P:j * P + r], w[:, k, :],
                                   start=(k == 0), stop=(k == KD - 1))
                mm.then_inc(out_done, 1)

            def turn_x1(j):
                r = ROWS[j]
                pe.wait_ge(x1_ready, j + 1)
                if j:
                    pe.wait_ge(x1T_act, j)
                    pe.wait_ge(x1T_dve, j)
                else:
                    pe.wait_ge(tail_kept, 2)
                for k in range(KD):
                    mm = pe.transpose(ps[:, 4 + k // 4, (k % 4) * r:(k % 4 + 1) * r], x_view[0:r, j, k, :],
                                      ident[0:r, 0:r])
                    if k % 4 == 3:
                        mm.then_inc(x1_turned, 1)

            def route(j):
                r = ROWS[j]
                pe.wait_ge(x1T_act, j + 1)
                pe.wait_ge(x1T_dve, j + 1)
                if j >= 2:
                    pe.wait_ge(logits_kept, j - 1)
                for k in range(KD):
                    mm = pe.matmul(ps[0:r, 6 + j % 2, 0:NR], x1T[:, k, 0:r], w_router[:, k, :],
                                   start=(k == 0), stop=(k == KD - 1))
                mm.then_inc(logits_done, 1)

            pe.wait_ge(in_dve, 8)
            pe.wait_ge(map_kept, NG)
            pe.wait_ge(wout_loaded[0], 16)
            for j in range(NT):
                out_project(0, j)
            pe.wait_ge(wout_loaded[1], 16)
            pe.wait_ge(router_loaded, 64)
            for j in range(3):
                out_project(1, j)
            turn_x1(0)
            out_project(1, 3)
            route(0)
            turn_x1(1)
            out_project(1, 4)
            route(1)
            for j in range(2, NT):
                turn_x1(j)
                route(j)

            pe.wait_ge(mask_ready, 1)
            for i in range(NT):
                for j in range(i + 1):
                    pe.matmul(ps[:, 0, i * E:(i + 1) * E], before[:, :] if j == i else ones[:, :], mask[:, j, :],
                              start=(j == 0), stop=(j == i))
            for j in range(NT):
                mm = pe.matmul(ps[:, 1, 0:E], ones[:, :], mask[:, j, :], start=(j == 0), stop=(j == NT - 1))
            mm.then_inc(pos_done, 1)

            pe.wait_ge(hot_ready, 1)
            for a in range(2 * NT):
                mm = pe.matmul(ps[0:SLOTS, 2, 0:2 * TILES], hot_col[:, a, :],
                               slot_val[:, a, :, :].rearrange("p b c -> p (b c)"), start=(a == 0), stop=(a == 2 * NT - 1))
            mm.then_inc(table_done, 1)

            def turn_tile(u, n):
                pe.wait_ge(gathered[u], n * 16 + 16)
                v = xe[u].rearrange("p (q k) -> p k q", k=KD)
                for k in range(KD):
                    mm = pe.transpose(ps[:, 4 + k // 4, (k % 4) * SLOTS:(k % 4 + 1) * SLOTS], v[0:SLOTS, k, :],
                                      ident[0:SLOTS, 0:SLOTS])
                    if k % 4 == 3:
                        mm.then_inc(xe_turned, 1)

            def hidden(u, n, seq):
                pe.wait_ge(w1_loaded[u], n * 16 + 16)
                pe.wait_ge(w3_loaded[u], n * 16 + 16)
                pe.wait_ge(xeT_act, seq + 1)
                pe.wait_ge(xeT_dve, seq + 1)
                for f in range(KF):
                    if f >= 2:
                        pe.wait_ge(h_ready, seq * KF + (f - 1))
                    for m, w in enumerate((w1_slot[u], w3_slot[u])):
                        for k in range(KD):
                            mm = pe.matmul(ps[:, f % 2, m * SLOTS:(m + 1) * SLOTS], w[:, k, f * P:(f + 1) * P],
                                           xeT[:, k, :], start=(k == 0), stop=(k == KD - 1))
                    mm.then_inc(h_done, 1)

            def down(u, n, seq):
                pe.wait_ge(w2_loaded[u], n * 16 + 16)
                wait(pe, ylo_kept, seq)
                wait(pe, yhi_kept, seq)
                for f in range(KF):
                    pe.wait_ge(h_ready, seq * KF + (f + 1))
                    for h in range(2):
                        mm = pe.matmul(ps[0:SLOTS, 2 + h, :], hT[:, f, :], w2_slot[u][:, f, h * 512:(h + 1) * 512],
                                       start=(f == 0), stop=(f == KF - 1))
                        if f == KF - 1:
                            mm.then_inc((ylo_done, yhi_done)[h], 1)

            def three_tiles(n):
                for u in range(RING):
                    seq = n * RING + u
                    hidden(u, n, seq)
                    turn_tile((u + 1) % RING, n + (u + 1) // RING)
                    down(u, n, seq)

            turn_tile(0, 0)
            three_tiles(0)
            with pe.Fori(1, E // RING) as n:
                three_tiles(n)
            n = E // RING
            hidden(0, n, E - 2)
            turn_tile(1, n)
            down(0, n, E - 2)
            hidden(1, n, E - 1)
            down(1, n, E - 1)

            pe.wait_ge(extra_ready, 1)
            n_extra = pe.value_load(extra[0:1, XTILES:XTILES + 1], min_val=0, max_val=XTILES)
            with pe.If(n_extra > 0):
                with pe.Fori(0, n_extra) as v:
                    pe.wait_ge(xeT_act, E + v)
                    pe.wait_ge(xeT_dve, E + v)
                    turn_tile(2, v + E // RING)
                    hidden(2, v + E // RING, v + E)
                    down(2, v + E // RING, v + E)

        @block.scalar
        def _(act):
            def copy(out, in_, **kw):
                return nc.scalar.activation(out, in_, ACT.Copy, **kw)

            turn_banks = [4, 5, 0, 1, 2, 3]
            for j in range(NT):
                r = ROWS[j]
                act.wait_ge(x_turned, 2 * j + 1)
                copy(xT[:, 0:4, j * P:j * P + r],
                     ps[:, turn_banks[(2 * j) % 6], 0:4 * r].rearrange("p (k t) -> p k t", k=4)).then_inc(xT_act, 1)

            def keep_values(g):
                act.wait_ge(in_done, g + 1)
                if g >= 2:
                    act.wait_ge(pooled_ready, g - 1)
                    act.wait_ge(vtail_kept, g - 1)
                b = 2 * (g % 2)
                v = vext[g % 2]
                copy(v[:, HIST:HIST + HALF], ps[:, b, 0:HALF])
                copy(v[:, HIST + HALF:PV], ps[:, b + 1, 0:SEQ - HALF])
                copy(v[:, PV:VEXT].rearrange("p (b t) -> p b t", b=NB)[:, :, HIST:],
                     ps[:, b + 1, SEQ - HALF:HALF].rearrange("p (b t) -> p b t", b=NB)).then_inc(in_act, 1)

            def keep_map(g):
                act.wait_ge(map_done, g + 1)
                nc.scalar.activation(mixT[:, g, 0:HALF], ps[:, 6, 0:HALF], ACT.Identity, scale=chan[:, g, 3:4])
                nc.scalar.activation(mixT[:, g, HALF:T], ps[:, 7, 0:HALF], ACT.Identity,
                                     scale=chan[:, g, 3:4]).then_inc(map_kept, 1)

            def keep_c(g):
                act.wait_ge(in_done, NG + g + 1)
                b = 2 * (g % 2)
                copy(mixT[:, NG + g, 0:HALF], ps[:, b, 0:HALF])
                copy(mixT[:, NG + g, HALF:T], ps[:, b + 1, 0:HALF]).then_inc(in_act, 1)

            keep_values(0)
            keep_values(1)
            keep_map(0)
            keep_values(2)
            keep_map(1)
            keep_values(3)
            keep_map(2)
            keep_c(0)
            keep_map(3)
            keep_c(1)
            act.wait_ge(pooled_ready, NG)
            act.wait_ge(tail_turned, 1)
            copy(wsum[0][0:HIST, 0:DP], ps[0:HIST, 4, :])
            copy(wsum[1][0:NB * HIST, 0:DP], ps[0:NB * HIST, 5, :]).then_inc(tail_kept, 1)
            act.wait_ge(tail_kept, 1)
            act.dma_start(pool_prompt[0], wsum[0][0:HIST, 0:DP]).then_inc(tail_stored, 16)
            act.dma_start(pool_sample.rearrange("b h c -> (b h) c"), wsum[1][0:NB * HIST, 0:DP]).then_inc(tail_stored, 16)
            keep_c(2)
            keep_c(3)
            act.wait_ge(tail_turned, 2)
            copy(pooled[0:CHIST, 0:DP], ps[0:CHIST, 4, :])
            copy(xeT_flat[0:NB * CHIST, 0:DP], ps[0:NB * CHIST, 5, :]).then_inc(tail_kept, 1)
            act.wait_ge(tail_kept, 2)
            act.dma_start(conv_prompt[0], pooled[0:CHIST, 0:DP]).then_inc(tail_stored, 16)
            act.dma_start(conv_sample.rearrange("b h c -> (b h) c"), xeT_flat[0:NB * CHIST, 0:DP]).then_inc(tail_stored, 16)

            def keep_x1T(j):
                r = ROWS[j]
                act.wait_ge(x1_turned, 2 * j + 1)
                if j:
                    act.wait_ge(logits_done, j)
                copy(x1T[:, 0:4, 0:r], ps[:, 4, 0:4 * r].rearrange("p (k t) -> p k t", k=4)).then_inc(x1T_act, 1)

            def deviation(n, r):
                act.wait_ge(var_ready, n + 1)
                nc.scalar.activation(std[0:r, :], mv[0:r, 1:2], ACT.Sqrt, bias=eps[0:r, :]).then_inc(std_ready, 1)

            act.wait_ge(consts_made, 2)
            deviation(0, P)
            deviation(1, P)
            for j in range(NT):
                if j + 2 < NT:
                    deviation(j + 2, ROWS[j + 2])
                act.wait_ge(x1_ready, j + 1)
                act.dma_start(x1_dram[j * P:j * P + ROWS[j], :], x_tok[0:ROWS[j], j, :]).then_inc(x1_stored, 16)
                keep_x1T(j)
            for n, (lo, hi) in enumerate(((0, 4), (4, 5))):
                r = ROWS[lo]
                act.wait_ge(diff_ready, 2 * n + 1)
                nc.scalar.activation(g_exp[0:r, lo:hi, :], g_tmp[0:r, lo:hi, :], ACT.Exp).then_inc(exp_ready, 1)
                act.wait_ge(diff_ready, 2 * n + 2)
                nc.scalar.activation(top[0:r, 3, lo:hi], top[0:r, 2, lo:hi], ACT.Exp).then_inc(exp_ready, 1)

            def keep_xeT(seq):
                act.wait_ge(xe_turned, seq * 2 + 1)
                copy(xeT[:, 0:4, :], ps[:, 4, 0:4 * SLOTS].rearrange("p (k t) -> p k t", k=4)).then_inc(xeT_act, 1)

            def silus(seq):
                for f in range(KF):
                    act.wait_ge(h_done, seq * KF + (f + 1))
                    if f >= 2:
                        act.wait_ge(h_ready, seq * KF + (f - 1))
                    nc.scalar.activation(silu[:, f % 2, :], ps[:, f % 2, 0:SLOTS], ACT.Silu).then_inc(silu_ready, 1)

            def keep_y(u, n, seq):
                wait(act, scattered[u], n * 16)
                act.wait_ge(ylo_done, seq + 1)
                copy(ye[u][0:SLOTS, 0:512], ps[0:SLOTS, 2, :]).then_inc(ylo_kept, 1)

            def three_tiles(n):
                for u in range(RING):
                    seq = n * RING + u
                    silus(seq)
                    keep_xeT(seq + 1)
                    keep_y(u, n, seq)

            keep_xeT(0)
            three_tiles(0)
            with act.Fori(1, E // RING) as n:
                three_tiles(n)
            n = E // RING
            silus(E - 2)
            keep_xeT(E - 1)
            keep_y(0, n, E - 2)
            silus(E - 1)
            keep_y(1, n, E - 1)

            act.wait_ge(extra_ready, 1)
            n_extra = act.value_load(extra[0:1, XTILES:XTILES + 1], min_val=0, max_val=XTILES)
            with act.If(n_extra > 0):
                with act.Fori(0, n_extra) as v:
                    keep_xeT(v + E)
                    silus(v + E)
                    keep_y(2, v + E // RING, v + E)

            for j in range(NT):
                r = ROWS[j]
                deviation(NT + j, r)
                act.wait_ge(stats_ready, j + 1)
                nc.scalar.activation(y_pair[0:r, j, 1, :], y_pair[0:r, j, 0, :], ACT.Identity,
                                     bias=rstd[0:r, 2 * (j % 2) + 1:2 * (j % 2) + 2],
                                     scale=rstd[0:r, 2 * (j % 2):2 * (j % 2) + 1]).then_inc(centred, 1)

        @block.gpsimd
        def _(pool):
            g = nc.gpsimd
            g.memset(ident[:, :], 0.0).then_inc(zeros_made, 1)
            g.memset(before[:, :], 1.0).then_inc(zeros_made, 1)
            pool.wait_ge(zeros_made, 2)
            g.affine_select(out=ident[:, :], in_=ident[:, :], compare_op=ALU.not_equal, fill=1.0, base=0,
                            pattern=[[-1, P]], channel_multiplier=1).then_inc(consts_made, 1)
            g.affine_select(out=before[:, :], in_=before[:, :], compare_op=ALU.is_gt, fill=0.0, base=0,
                            pattern=[[1, P]], channel_multiplier=-1)
            for i in range(2):
                g.memset(vext[i][:, 0:HIST], 0.0)
            g.iota(counts, [[1, HIST]], base=1, channel_multiplier=0,
                   allow_small_or_imprecise_dtypes=True).then_inc(zeros_made, 1)
            g.memset(ones[:, :], 1.0)
            g.memset(eps[:, :], EPS)
            g.memset(logits[:, NT - 1, :], 0.0)
            g.iota(iota[:, :], [[1, SLOTS]], base=0, channel_multiplier=0, allow_small_or_imprecise_dtypes=True)
            g.iota(rev[:, :], [[-1, EPG]], base=EPG, channel_multiplier=0, allow_small_or_imprecise_dtypes=True)
            g.iota(edges[:, :], [[SLOTS, NQ]], base=SLOTS, channel_multiplier=0, allow_small_or_imprecise_dtypes=True)
            g.iota(tokval[:, :, 0], [[P, NT]], base=1, channel_multiplier=1, allow_small_or_imprecise_dtypes=True)
            g.iota(tokval[:, :, 1:3], [[2 * P, NT], [1, 2]], base=1, channel_multiplier=2,
                   allow_small_or_imprecise_dtypes=True).then_inc(zeros_made, 1)
            pool.wait_ge(zeros_made, 4)
            g.memset(tokval[64:P, NT - 1, :], 0.0).then_inc(consts_made, 1)
            pool.wait_ge(consts_made, 2)

            for c in range(NG):
                v = vext[c % 2]
                pool.wait_ge(in_act, c + 1)
                g.tensor_copy(vtail[:, c, 0:HIST], v[:, PV - HIST:PV])
                pool.wait_ge(pooled_ready, c + 1)
                g.tensor_copy(vtail[:, c, HIST:VTAIL].rearrange("p (b t) -> p b t", b=NB),
                              v[:, PV:VEXT].rearrange("p (b t) -> p b t", b=NB)[:, :, NS:]).then_inc(vtail_kept, 1)
            for c in range(NG):
                pool.wait_ge(in_dve, c + 1)
                v = vext[c % 2]
                g.tensor_copy(utail[:, c, 0:CHIST], v[:, PU - CHIST:PU])
                g.tensor_copy(utail[:, c, CHIST:UTAIL].rearrange("p (b t) -> p b t", b=NB),
                              v[:, PU:UEXT].rearrange("p (b t) -> p b t", b=NB)[:, :, NS:]).then_inc(utail_kept, 1)
            pool.wait_ge(ln1_loaded, 32)
            for j in range(NT):
                r = ROWS[j]
                pool.wait_ge(x1_scaled, j + 1)
                g.tensor_tensor(x_tok[0:r, j, :], x_tok[0:r, j, :], ln1[0:r, 1, :], ALU.add).then_inc(x1_ready, 1)

            last_token, last_output = pool.to_reg(T - 1), pool.to_reg(2 * T - 1)

            def gather(u, n, seq, used):
                wait(pool, gathered[u], n * 16)
                g.tensor_copy(gather_idx[0:SLOTS, u:u + 1],
                              slot_rows[0:SLOTS, 0, bass.DynSlice(seq, 1)]).then_inc(gather_col, 1)
                pool.wait_ge(gather_col, seq + 1)
                wait(pool, xe_turned, used * 2)
                pool.sem_inc(issued, 1)
                g.indirect_dma_start(out=xe[u][0:SLOTS, :], out_offset=None, in_=x1_dram[:, :],
                                     in_offset=bass.IndirectOffsetOnAxis(ap=gather_idx[0:SLOTS, u:u + 1], axis=0),
                                     bounds_check=last_token, oob_is_err=False).then_inc(gathered[u], 16)

            def scatter(u, n, seq):
                wait(pool, scattered[u], n * 16)
                g.tensor_copy(scatter_idx[0:SLOTS, u:u + 1],
                              slot_rows[0:SLOTS, 1, bass.DynSlice(seq, 1)]).then_inc(scatter_col, 1)
                pool.wait_ge(scatter_col, seq + 1)
                pool.wait_ge(ylo_kept, seq + 1)
                pool.wait_ge(yhi_kept, seq + 1)
                pool.sem_inc(issued, 1)
                g.indirect_dma_start(out=y_dram[:, :],
                                     out_offset=bass.IndirectOffsetOnAxis(ap=scatter_idx[0:SLOTS, u:u + 1], axis=0),
                                     in_=ye[u][0:SLOTS, :], in_offset=None,
                                     bounds_check=last_output, oob_is_err=False).then_inc(scattered[u], 16)

            pool.wait_ge(table_ready, 1)
            pool.wait_ge(x1_stored, 16 * NT)
            gather(0, 0, 0, 0)
            gather(1, 0, 1, 0)
            def three_tiles(n):
                for u in range(RING):
                    seq = n * RING + u
                    gather((u + 2) % RING, n + (u + 2) // RING, seq + 2, seq)
                    scatter(u, n, seq)

            three_tiles(0)
            with pool.Fori(1, E // RING) as n:
                three_tiles(n)
            scatter(0, E // RING, E - 2)
            scatter(1, E // RING, E - 1)

            pool.wait_ge(extra_ready, 1)
            n_extra = pool.value_load(extra[0:1, XTILES:XTILES + 1], min_val=0, max_val=XTILES)
            with pool.If(n_extra > 0):
                with pool.Fori(0, n_extra) as v:
                    gather(2, v + E // RING, v + E, v + E)
                    scatter(2, v + E // RING, v + E)

            pool.wait_ge(ln2_loaded, 32)
            for j in range(NT):
                r = ROWS[j]
                pool.wait_ge(centred, j + 1)
                g.tensor_tensor(y_pair[0:r, j, 1, :], y_pair[0:r, j, 1, :], ln2[0:r, 0, :], ALU.mult).then_inc(gained, 1)

        @block.vector
        def _(dve):
            v = nc.vector
            steps = [0]
            deviations = [0]

            def settled(ins):
                steps[0] += 1
                ins.then_inc(step, 1)
                dve.wait_ge(step, steps[0])

            turn_banks = [4, 5, 0, 1, 2, 3]
            for j in range(NT):
                r = ROWS[j]
                dve.wait_ge(x_turned, 2 * j + 2)
                v.tensor_copy(xT[:, 4:8, j * P:j * P + r],
                              ps[:, turn_banks[(2 * j + 1) % 6], 0:4 * r].rearrange("p (k t) -> p k t", k=4)
                              ).then_inc(xT_dve, 1)
            dve.wait_ge(rows_turned, 1)
            v.tensor_copy(poolT, ps[:, 6, 0:480].rearrange("p (j t) -> p j t", j=NG)).then_inc(rows_kept, 1)
            dve.wait_ge(rows_turned, 2)
            v.tensor_copy(chan[:, :, :], ps[:, 7, 0:16].rearrange("p (j t) -> p j t", j=NG))
            v.tensor_copy(convT, ps[:, 7, 16:80].rearrange("p (j t) -> p j t", j=NG)).then_inc(rows_kept, 1)
            dve.wait_ge(rows_kept, 2)
            dve.wait_ge(zeros_made, 3)
            settled(v.reciprocal(counts, counts))

            for c in range(NG):
                w = 2 << c
                val = vext[c % 2]
                sample = val[:, PV:VEXT].rearrange("p (b t) -> p b t", b=NB)
                if c >= 2:
                    dve.wait_ge(vtail_kept, c - 1)
                settled(v.tensor_copy(sample[:, :, 0:HIST], poolT[:, c, :].rearrange("p (b t) -> p b t", b=NB)))
                dve.wait_ge(in_act, c + 1)
                src, reach = val, 1
                for s in range(c + 1):
                    dst = wsum[s % 2]
                    lo = 2 * reach - 1
                    settled(v.tensor_tensor(dst[:, lo:VEXT], src[:, lo:VEXT], src[:, lo - reach:VEXT - reach], ALU.add))
                    src, reach = dst, 2 * reach
                if c:
                    dve.wait_ge(map_done, c)
                ssum = src[:, PV:VEXT].rearrange("p (b t) -> p b t", b=NB)
                v.scalar_tensor_tensor(pooled[:, w - 1:SEQ], src[:, HIST + w - 1:PV], 1.0 / w,
                                       val[:, HIST + w - 1:PV], ALU.mult, ALU.subtract)
                v.scalar_tensor_tensor(pooled[:, SEQ:T].rearrange("p (b t) -> p b t", b=NB), ssum[:, :, HIST:], 1.0 / w,
                                       sample[:, :, HIST:], ALU.mult, ALU.subtract)
                settled(v.tensor_tensor(pooled[:, 0:w - 1], src[:, HIST:HIST + w - 1], counts[:, 0:w - 1], ALU.mult))
                v.tensor_tensor(pooled[:, 0:w - 1], pooled[:, 0:w - 1], val[:, HIST:HIST + w - 1],
                                ALU.subtract).then_inc(pooled_ready, 1)

            for c in range(NG):
                b = 2 * (c % 2)
                u = vext[c % 2]
                us = u[:, PU:UEXT].rearrange("p (b t) -> p b t", b=NB)
                gate = mixT[:, NG + c, :]
                if c < 2:
                    dve.wait_ge(vtail_kept, NG)
                else:
                    dve.wait_ge(utail_kept, c - 1)
                v.tensor_copy(us[:, :, 0:CHIST], convT[:, c, :].rearrange("p (b t) -> p b t", b=NB))
                dve.wait_ge(in_act, NG + c + 1)
                dve.wait_ge(in_done, 2 * NG + c + 1)
                v.tensor_tensor(u[:, CHIST:CHIST + HALF], gate[:, 0:HALF], ps[:, b, 0:HALF], ALU.mult)
                v.tensor_tensor(u[:, CHIST + HALF:PU], gate[:, HALF:SEQ], ps[:, b + 1, 0:SEQ - HALF], ALU.mult)
                settled(v.tensor_tensor(us[:, :, CHIST:], gate[:, SEQ:T].rearrange("p (b t) -> p b t", b=NB),
                                        ps[:, b + 1, SEQ - HALF:HALF].rearrange("p (b t) -> p b t", b=NB), ALU.mult))
                dve.sem_inc(in_dve, 1)
                gp, gs = gate[:, 0:SEQ], gate[:, SEQ:T].rearrange("p (b t) -> p b t", b=NB)
                v.tensor_scalar(gp, u[:, 0:SEQ], chan[:, c, 0:1], None, ALU.mult)
                settled(v.tensor_scalar(gs, us[:, :, 0:NS], chan[:, c, 0:1], None, ALU.mult))
                for k in (1, 2):
                    v.scalar_tensor_tensor(gp, u[:, k:SEQ + k], chan[:, c, k:k + 1], gp, ALU.mult, ALU.add)
                    settled(v.scalar_tensor_tensor(gs, us[:, :, k:NS + k], chan[:, c, k:k + 1], gs, ALU.mult, ALU.add))
            for c in range(NG):
                b = 2 * (c % 2)
                dve.wait_ge(in_done, 3 * NG + c + 1)
                v.tensor_tensor(mixT[:, NG + c, 0:HALF], mixT[:, NG + c, 0:HALF], ps[:, b, 0:HALF], ALU.mult)
                v.tensor_tensor(mixT[:, NG + c, HALF:T], mixT[:, NG + c, HALF:T], ps[:, b + 1, 0:HALF],
                                ALU.mult).then_inc(in_dve, 1)

            def residual(h, j):
                o, r = h * NT + j, ROWS[j]
                dve.wait_ge(out_done, o + 1)
                if h == 0:
                    dve.wait_ge(xT_act, NT)
                x = x_tok[0:r, j, h * 512:(h + 1) * 512]
                return v.scalar_tensor_tensor(x, x, ALPHA, ps[0:r, o % 4, :], ALU.mult, ALU.add)

            def normal(row, r, scale, bias=None):
                v.bn_stats(stats[0:r, 0, :], row[:, 0:512])
                settled(v.bn_stats(stats[0:r, 1, :], row[:, 512:D]))
                settled(v.bn_aggr(mv[0:r, :], stats[0:r, :, :].rearrange("p a b -> p (a b)")))
                dve.sem_inc(var_ready, 1)
                deviations[0] += 1
                dve.wait_ge(std_ready, deviations[0])
                settled(v.reciprocal(scale, std[0:r, :]))
                if bias is not None:
                    return v.scalar_tensor_tensor(bias, mv[0:r, 0:1], -1.0, scale, ALU.mult, ALU.mult)

            def norm1(j):
                r = ROWS[j]
                settled(residual(1, j))
                dve.sem_inc(out_kept, 1)
                row = x_tok[0:r, j, :]
                normal(row, r, rstd[0:r, 0:1])
                settled(v.tensor_scalar(row, row, mv[0:r, 0:1], rstd[0:r, 0:1], ALU.subtract, ALU.mult))
                v.tensor_tensor(row, row, ln1[0:r, 0, :], ALU.mult).then_inc(x1_scaled, 1)

            def keep_x1T(j):
                r = ROWS[j]
                dve.wait_ge(x1_turned, 2 * j + 2)
                if j:
                    dve.wait_ge(logits_done, j)
                v.tensor_copy(x1T[:, 4:8, 0:r], ps[:, 5, 0:4 * r].rearrange("p (k t) -> p k t", k=4)).then_inc(x1T_dve, 1)

            def keep_logits(j):
                r = ROWS[j]
                dve.wait_ge(logits_done, j + 1)
                v.tensor_tensor(logits[0:r, j, :], ps[0:r, 6 + j % 2, 0:NR], b_router[0:r, :], ALU.add).then_inc(logits_kept, 1)

            for j in range(NT):
                residual(0, j).then_inc(out_kept, 1)
            dve.wait_ge(ln1_loaded, 32)
            dve.wait_ge(router_loaded, 64)
            dve.wait_ge(consts_made, 2)
            norm1(0)
            norm1(1)
            norm1(2)
            keep_x1T(0)
            norm1(3)
            keep_logits(0)
            keep_x1T(1)
            norm1(4)
            keep_logits(1)
            for j in range(2, NT - 1):
                keep_x1T(j)
                keep_logits(j)
            dve.wait_ge(out_done, 2 * NT)
            settled(v.memset(picked[:, NT - 1, :, :], 0.0))

            def choose(lo, hi, n_, src, largest, hot, tmp):
                r, m = ROWS[lo], hi - lo
                wide = [r, m, n_]
                settled(v.tensor_reduce(largest, src, AX.X, ALU.max))
                settled(v.tensor_tensor(tmp, src, largest.unsqueeze(2).to_broadcast(wide), ALU.is_equal))
                settled(v.tensor_tensor(tmp, tmp, rev[0:r, 0:n_].unsqueeze(1).to_broadcast(wide), ALU.mult))
                settled(v.tensor_reduce(best[0:r, lo:hi], tmp, AX.X, ALU.max))
                settled(v.tensor_tensor(hot, tmp, best[0:r, lo:hi].unsqueeze(2).to_broadcast(wide), ALU.is_equal))

            def choose_experts(n, lo, hi):
                r, m = ROWS[lo], hi - lo
                lg = logits[0:r, lo:hi, 0:EG]
                le = logits[0:r, lo:hi, EG:NR].rearrange("p n (g e) -> p n g e", g=EG)
                gmax, m1, m2, ex = [top[0:r, i, lo:hi] for i in range(4)]
                gh, ev = g_hot[0:r, lo:hi, :], e_val[0:r, lo:hi, :]
                choose(lo, hi, EG, lg, gmax, gh, g_tmp[0:r, lo:hi, :])
                v.tensor_tensor(g_tmp[0:r, lo:hi, :], lg, gmax.unsqueeze(2).to_broadcast([r, m, EG]),
                                ALU.subtract).then_inc(diff_ready, 1)
                lsel = in_group[0:r, lo:hi, :].rearrange("p n (g e) -> p n g e", g=EG)
                settled(v.tensor_tensor(lsel, le, gh.unsqueeze(3).to_broadcast([r, m, EG, EPG]), ALU.mult))
                settled(v.tensor_reduce(ev, lsel.rearrange("p n g e -> p n e g"), AX.X, ALU.add))
                h1, h2 = e_hot[0:r, lo:hi, 0, :], e_hot[0:r, lo:hi, 1, :]
                choose(lo, hi, EPG, ev, m1, h1, e_tmp[0:r, lo:hi, :])
                settled(v.scalar_tensor_tensor(ev, h1, -3.0e38, ev, ALU.mult, ALU.add))
                choose(lo, hi, EPG, ev, m2, h2, e_tmp[0:r, lo:hi, :])
                v.tensor_tensor(m2, m2, m1, ALU.subtract).then_inc(diff_ready, 1)
                for k in range(2):
                    pk = picked[0:r, lo:hi, k, :].rearrange("p n (g e) -> p n g e", g=EG)
                    settled(v.tensor_tensor(pk, gh.unsqueeze(3).to_broadcast([r, m, EG, EPG]),
                                            e_hot[0:r, lo:hi, k, :].unsqueeze(2).to_broadcast([r, m, EG, EPG]), ALU.mult))

            def gate_values(n, lo, hi):
                r = ROWS[lo]
                gmax, m1, m2, ex = [top[0:r, i, lo:hi] for i in range(4)]
                dve.wait_ge(exp_ready, 2 * n + 2)
                settled(v.tensor_reduce(best[0:r, lo:hi], g_exp[0:r, lo:hi, :], AX.X, ALU.add))
                settled(v.tensor_scalar(lift[0:r, lo:hi], ex, 1.0, None, ALU.add))
                settled(v.tensor_tensor(lift[0:r, lo:hi], lift[0:r, lo:hi], best[0:r, lo:hi], ALU.mult))
                settled(v.reciprocal(gates[0:r, lo:hi, 0], lift[0:r, lo:hi]))
                settled(v.tensor_tensor(gates[0:r, lo:hi, 1], gates[0:r, lo:hi, 0], ex, ALU.mult))

            choose_experts(0, 0, 4)
            gate_values(0, 0, 4)
            keep_x1T(NT - 1)
            keep_logits(NT - 1)
            dve.wait_ge(logits_kept, NT)
            choose_experts(1, 4, 5)
            v.tensor_tensor(mask, picked[:, :, 0, :], picked[:, :, 1, :], ALU.add).then_inc(mask_ready, 1)
            gate_values(1, 4, 5)

            pick = picked.rearrange("p n k e -> p (n k) e")
            prod = product.rearrange("p n k e -> p (n k) e")
            A = 2 * NT

            def row(x, n):
                return x.unsqueeze(1).to_broadcast([P, n, x.shape[-1]])

            settled(v.tensor_tensor(prod, pick, row(iota[:, 0:E], A), ALU.mult))
            settled(v.tensor_reduce(expert, prod, AX.X, ALU.add))
            dve.wait_ge(pos_done, 1)
            settled(v.tensor_copy(cnt, ps[:, 1, 0:E]))
            settled(v.tensor_tensor(past_cnt, cnt.unsqueeze(2).to_broadcast([P, E, NQ]), row(edges[:, :], E), ALU.is_gt))
            settled(v.tensor_reduce(further, past_cnt, AX.X, ALU.add))
            settled(v.tensor_tensor_scan(upto, ones[:, 0:E], further, 0.0, ALU.mult, ALU.add))
            settled(v.tensor_tensor(first, upto, further, ALU.subtract))
            settled(v.tensor_tensor(prod, pick, row(first, A), ALU.mult))
            settled(v.tensor_reduce(base, prod, AX.X, ALU.add))
            settled(v.tensor_tensor(product, picked, ps[:, 0, 0:NT * E].rearrange("p (n e) -> p n e", n=NT)
                                    .unsqueeze(2).to_broadcast([P, NT, 2, E]), ALU.mult))
            settled(v.tensor_reduce(pos, prod, AX.X, ALU.add))
            settled(v.tensor_tensor(past_pos, pos.unsqueeze(2).to_broadcast([P, A, NQ]), row(edges[:, :], A), ALU.is_ge))
            settled(v.tensor_reduce(quot, past_pos, AX.X, ALU.add))
            settled(v.scalar_tensor_tensor(col, quot, -float(SLOTS), pos, ALU.mult, ALU.add))
            settled(v.tensor_tensor(base, base, quot, ALU.add))
            settled(v.tensor_tensor(base, base, expert, ALU.subtract))
            settled(v.tensor_scalar(base, base, float(E - 1), None, ALU.add))
            settled(v.scalar_tensor_tensor(tile_no, quot, 0.0, base, ALU.is_gt, ALU.mult))
            settled(v.tensor_tensor(tile_no, tile_no, expert, ALU.add))
            v.tensor_tensor(hot_col, row(iota[:, :], A), col.unsqueeze(2).to_broadcast([P, A, SLOTS]), ALU.is_equal)
            settled(v.tensor_tensor(hot_tile, row(iota[:, 0:TILES], A),
                                    tile_no.unsqueeze(2).to_broadcast([P, A, TILES]), ALU.is_equal))
            hot4 = hot_tile.rearrange("p (n k) c -> p n k c", k=2)
            val5 = slot_val.rearrange("p (n k) b c -> p n k b c", k=2)
            for k in range(2):
                v.tensor_tensor(val5[:, :, k, 0, :], hot4[:, :, k, :],
                                tokval[:, :, 0].unsqueeze(2).to_broadcast([P, NT, TILES]), ALU.mult)
                last = v.tensor_tensor(val5[:, :, k, 1, :], hot4[:, :, k, :],
                                       tokval[:, :, 1 + k].unsqueeze(2).to_broadcast([P, NT, TILES]), ALU.mult)
            last.then_inc(hot_ready, 1)
            settled(v.tensor_tensor(over[0:1], upto[0:1].unsqueeze(1).to_broadcast([1, XTILES, E]),
                                    iota[0:1, 0:XTILES].unsqueeze(2).to_broadcast([1, XTILES, E]), ALU.is_le))
            settled(v.tensor_reduce(over_n[0:1], over[0:1], AX.X, ALU.add))
            v.tensor_scalar(extra[0:1, 0:XTILES], over_n[0:1], float(E - 1), None, ALU.min)
            v.tensor_copy(extra[0:1, XTILES:XTILES + 1], upto[0:1, E - 1:E]).then_inc(extra_ready, 1)
            dve.wait_ge(table_done, 1)
            table = ps[0:SLOTS, 2, 0:2 * TILES]
            empty = in_group.rearrange("p a b -> p (a b)")[0:SLOTS, 0:2 * TILES]
            settled(v.tensor_scalar(empty, table, 0.0, float(PAD), ALU.is_equal, ALU.mult))
            v.scalar_tensor_tensor(slot_rows[0:SLOTS, :, :].rearrange("p a b -> p (a b)"), table, -1.0, empty,
                                   ALU.add, ALU.add).then_inc(table_ready, 1)
            dve.wait_ge(x1_stored, 16 * NT)
            for j in range(NT):
                v.tensor_scalar(x_tok[0:ROWS[j], j, :], x_tok[0:ROWS[j], j, :], ALPHA, None, ALU.mult)

            def keep_xeT(seq):
                dve.wait_ge(xe_turned, seq * 2 + 2)
                v.tensor_copy(xeT[:, 4:8, :], ps[:, 5, 0:4 * SLOTS].rearrange("p (k t) -> p k t", k=4)).then_inc(xeT_dve, 1)

            def products(seq):
                for f in range(KF):
                    dve.wait_ge(silu_ready, seq * KF + (f + 1))
                    v.tensor_tensor(hT[:, f, :], silu[:, f % 2, :], ps[:, f % 2, SLOTS:2 * SLOTS],
                                    ALU.mult).then_inc(h_ready, 1)

            def keep_y(u, n, seq):
                wait(dve, scattered[u], n * 16)
                dve.wait_ge(yhi_done, seq + 1)
                v.tensor_copy(ye[u][0:SLOTS, 512:D], ps[0:SLOTS, 3, :]).then_inc(yhi_kept, 1)

            def three_tiles(n):
                for u in range(RING):
                    seq = n * RING + u
                    products(seq)
                    keep_xeT(seq + 1)
                    keep_y(u, n, seq)

            keep_xeT(0)
            three_tiles(0)
            with dve.Fori(1, E // RING) as n:
                three_tiles(n)
            n = E // RING
            products(E - 2)
            keep_xeT(E - 1)
            keep_y(0, n, E - 2)
            products(E - 1)
            keep_y(1, n, E - 1)

            n_extra = dve.value_load(extra[0:1, XTILES:XTILES + 1], min_val=0, max_val=XTILES)
            with dve.If(n_extra > 0):
                with dve.Fori(0, n_extra) as i:
                    keep_xeT(i + E)
                    products(i + E)
                    keep_y(2, i + E // RING, i + E)

            def finish(j):
                r = ROWS[j]
                dve.wait_ge(gained, j + 1)
                v.tensor_tensor(y_pair[0:r, j, 0, :], y_pair[0:r, j, 1, :], ln2[0:r, 1, :], ALU.add).then_inc(out_ready, 1)

            for j in range(NT):
                r = ROWS[j]
                a, b = y_pair[0:r, j, 0, :], y_pair[0:r, j, 1, :]
                dve.wait_ge(y_loaded[j], 16)
                settled(v.scalar_tensor_tensor(a, a, gates[0:r, j, 0:1], x_tok[0:r, j, :], ALU.mult, ALU.add))
                settled(v.scalar_tensor_tensor(a, b, gates[0:r, j, 1:2], a, ALU.mult, ALU.add))
                i = 2 * (j % 2)
                if j >= 2:
                    dve.wait_ge(centred, j - 1)
                normal(a, r, rstd[0:r, i:i + 1], rstd[0:r, i + 1:i + 2]).then_inc(stats_ready, 1)
                if j:
                    finish(j - 1)
            dve.wait_ge(ln2_loaded, 32)
            finish(NT - 1)


_INS = ["x_prompt", "x_sample", "state_pool", "state_conv", "w_in", "w_pool_map", "pool_scale", "conv_w", "w_out",
        "ln1_g", "ln1_b", "w_group", "b_group", "w_expert", "b_expert", "w1", "w3", "w2", "ln2_g", "ln2_b"]
_OUTS = [(1, SEQ, D), (NB, NS, D), (1, HIST, DP), (1, CHIST, DP), (NB, HIST, DP), (NB, CHIST, DP)]


def kernel(**inputs):
    import numpy as np
    import concourse.bacc as bacc
    from concourse.bass_utils import run_bass_kernel_spmd

    nc = bacc.Bacc("TRN2", target_bir_lowering=False, num_devices=1)
    arrays, args = {}, []
    for name in _INS:
        a = np.ascontiguousarray(inputs[name])
        arrays[f"in_{name}"] = a
        args.append(nc.dram_tensor(f"in_{name}", a.shape, mybir.dt.from_np(a.dtype), kind="ExternalInput").ap())
    for i, shape in enumerate(_OUTS):
        args.append(nc.dram_tensor(f"out_{i}", shape, F32, kind="ExternalOutput").ap())
    build(nc, *args)
    r = run_bass_kernel_spmd(nc, [arrays], core_ids=[0])
    return tuple(r.results[0][f"out_{i}"] for i in range(len(_OUTS)))
```

```python
from contextlib import ExitStack

import concourse.bass as bass
from concourse import mybir

F32 = mybir.dt.float32
F32R = mybir.dt.float32r
BF16 = mybir.dt.bfloat16
I32 = mybir.dt.int32
ALU = mybir.AluOpType
ACT = mybir.ActivationFunctionType
AX = mybir.AxisListType

P = 128
D = 1024
KD = D // P
SEQ = 512
NB, NS = 8, 8
T = SEQ + NB * NS
HALF = T // 2
NT = 5
ROWS = [P, P, P, P, NB * NS]
DP = 512
NG = DP // P
HIST, CHIST = 15, 2
PV = HIST + SEQ
VEXT = PV + NB * (HIST + NS)
PU = CHIST + SEQ
UEXT = PU + NB * (CHIST + NS)
VTAIL = HIST * (1 + NB)
UTAIL = CHIST * (1 + NB)
EG, EPG = 4, 8
E = EG * EPG
NR = EG + E
F = 512
KF = F // P
SLOTS = 64
XTILES = (2 * T) // SLOTS
TILES = E + XTILES
NQ = (T - 1) // SLOTS
ALPHA = 2.0 ** 0.25
EPS = 1e-5
RING = 3
BLK = KD * F
FH = F // 2
DH = D // 2
KH = KD // 2
B1, B3, BY, BX, BXT, BHT = range(6)


def build(nc, x_prompt, x_sample, state_pool, state_conv, w_in, w_pool_map, pool_scale, conv_w, w_out,
          ln1_g, ln1_b, w_group, b_group, w_expert, b_expert, w1, w3, w2, ln2_g, ln2_b,
          y_prompt, y_sample, pool_prompt, conv_prompt, pool_sample, conv_sample):
    ctx = ExitStack()
    with ctx:
        def sb(name, shape, dt=F32):
            return ctx.enter_context(nc.sbuf_tensor(name, shape, dt))

        def sem(name):
            return ctx.enter_context(nc.semaphore(name))

        def parts(stack, name, *shape):
            return stack.enter_context(nc.sbuf_tensor(name, [P, *shape], F32R))

        sums_dram = nc.dram_tensor("expert_sums", (T + SLOTS, D), F32).ap()

        x_tok = sb("x_tok", [P, NT, D])
        with ExitStack() as early:
            xT = [parts(early, f"xT_{part}", KD, T) for part in ("high", "low")]
            w_part = [parts(early, f"w_in_{part}", 2, KD, P) for part in ("high", "low")]
            mix_high = parts(early, "mix_high", KD, T)
            parts(early, "untouched", 6 * BLK - 3 * KD * T - 4 * KD * P)
            wout_high0 = parts(early, "w_out_high0", KD, DP)
            wout_low = [parts(early, f"w_out_low{h}", KD, DP) for h in range(2)]
        with ExitStack() as early:
            wout_high1 = parts(early, "w_out_high1", KD, DP)
        wout_part = [[wout_high0, wout_low[0]], [wout_high1, wout_low[1]]]
        blocks = sb("blocks", [P, 9, BLK])
        with ExitStack() as early:
            mix_low = parts(early, "mix_low", KD, T)
        mix_part = [mix_high, mix_low]
        io = sb("io", [P, 6, D])
        equal = sb("equal", [P, 2 * NT, SLOTS])
        w_router = sb("w_router", [P, KD, NR])
        b_router = sb("b_router", [P, NR])
        ln1 = sb("ln1", [P, 2, D])
        ident = sb("ident", [P, P])
        before = sb("before", [P, P], BF16)
        ones = sb("ones", [P, P], BF16)
        iota = sb("iota", [P, SLOTS])
        rev = sb("rev", [P, EPG])
        edges = sb("edges", [P, NQ])
        tokval = sb("tokval", [P, NT])
        pad_row = sb("pad_row", [P, 1])
        chan = sb("chan", [P, NG, 4])
        w_map = sb("w_map", [P, NG, P])
        logits = sb("logits", [P, NT, NR])
        stats = sb("stats", [P, 2, 6])
        mv = sb("mv", [P, 2])
        rstd = sb("rstd", [P, NT, 2])
        std = sb("std", [P, 1])
        eps = sb("eps", [P, 2])
        gates = sb("gates", [P, NT, 2])
        rel = sb("rel", [P, 2 * NT])
        slot_row = sb("slot_row", [P, TILES], I32)
        slot_gate = sb("slot_gate", [P, TILES])
        scatter_idx = sb("scatter_idx", [P, 1], I32)
        extra = sb("extra", [1, XTILES + 1], I32)

        w1_slot = [blocks[:, b, :].rearrange("p (k f) -> p k f", k=KD) for b in (0, 3, 7)]
        w3_slot = [blocks[:, b, :].rearrange("p (k f) -> p k f", k=KD) for b in (1, 4, 8)]
        w2_slot = [blocks[:, b, :].rearrange("p (k d) -> p k d", k=KF) for b in (2, 5, 6)]
        ye = [io[:, u, :] for u in range(RING)]

        win_a = blocks[:, 7, :].rearrange("p (k c) -> p k c", k=KD)
        win_b = blocks[:, 8, :].rearrange("p (k c) -> p k c", k=KD)
        area = blocks[:, 5:7, :].rearrange("p a b -> p (a b)")
        at = 0
        vext = [area[:, at + i * VEXT:at + (i + 1) * VEXT] for i in range(2)]
        wsum = [area[:, at + (2 + i) * VEXT:at + (3 + i) * VEXT] for i in range(2)]
        pooled = area[:, at + 4 * VEXT:at + 4 * VEXT + T]
        io_flat = io[:, :, :].rearrange("p a b -> p (a b)")
        mixT = io_flat[:, 0:2 * NG * T].rearrange("p (j t) -> p j t", j=2 * NG)
        at = 2 * NG * T
        x1T = io_flat[:, at:at + D].rearrange("p (k t) -> p k t", k=KD)
        vtail = io_flat[:, at:at + NG * VTAIL].rearrange("p (j t) -> p j t", j=NG)
        at += NG * VTAIL
        poolT = io_flat[:, at:at + NG * NB * HIST].rearrange("p (j t) -> p j t", j=NG)
        at += NG * NB * HIST
        convT = io_flat[:, at:at + NG * NB * CHIST].rearrange("p (j t) -> p j t", j=NG)
        at += NG * NB * CHIST
        utail = io_flat[:, at:at + NG * UTAIL].rearrange("p (j t) -> p j t", j=NG)
        equal_flat = equal[:, :, :].rearrange("p a c -> p (a c)")
        pool_rows = ln1[:, 0, 0:DP]
        conv_rows = ln1[:, 0, DP:2 * DP]
        chan_rows = ln1[:, 1, 0:DP]
        counts = equal_flat[:, 0:HIST]

        at = 2 * NG * T
        silu = io_flat[:, at:at + FH]
        h_rows = io_flat[:, at + FH:at + 2 * FH]
        hT = io_flat[:, at + 2 * FH:at + 3 * FH].rearrange("p (c s) -> p c s", c=2)
        xe = ln1[:, 0, 0:DH]
        xeT = ln1[:, 0, DH:2 * DH].rearrange("p (c s) -> p c s", c=KH)
        hot = [ln1[:, 1, i * NT * SLOTS:(i + 1) * NT * SLOTS].rearrange("p (j c) -> p j c", j=NT) for i in range(RING)]

        def router_memory():
            areas = [[3 * D, 2 * NG * T], [2 * NG * T + D, 6 * D]]

            def take(*shape):
                n = 1
                for s in shape:
                    n *= s
                a = next(a for a in areas if a[0] + n <= a[1])
                a[0] += n
                v = io_flat[:, a[0] - n:a[0]]
                names = ["a", "b", "c", "d"][:len(shape)]
                if len(shape) > 1:
                    v = v.rearrange(f"p ({' '.join(names)}) -> p {' '.join(names)}",
                                    **dict(zip(names[1:], shape[1:])))
                return v
            return take

        take = router_memory()
        picked = take(NT, 2, E)
        product = take(NT, 2, E)
        mask = take(NT, E // 2).bitcast(BF16)
        in_group = take(NT, E)
        past_cnt = take(E, NQ)
        past_pos = take(NT * 2, NQ)
        g_hot, g_tmp, g_exp = take(NT, EG), take(NT, EG), take(NT, EG)
        e_val, e_tmp = take(NT, EPG), take(NT, EPG)
        e_hot = take(NT, 2, EPG)
        top = take(4, NT)
        best = take(NT)
        lift = take(NT)
        cnt, further, upto, first = take(E), take(E), take(E), take(E)
        pos, quot, base, expert, tile_no, col = [take(NT * 2) for _ in range(6)]
        hot_col = io_flat[:, 0:640].rearrange("p (a c) -> p a c", a=10)
        hot_tile = io_flat[:, 640:640 + 10 * TILES].rearrange("p (a c) -> p a c", a=10)
        slot_val = io_flat[:, 1140:1140 + 20 * TILES].rearrange("p (a b c) -> p a b c", a=10, b=2)
        over = io_flat[:, 2140:2140 + XTILES * E].rearrange("p (a e) -> p a e", a=XTILES)
        over_n = take(XTILES)

        SHARED = 2
        head = blocks[:, 0:3, :].rearrange("p a b -> p (a b)")
        total = head[:, 0:NT * D].rearrange("p (j d) -> p j d", j=NT)
        normed = head[:, NT * D:NT * 2 * D].rearrange("p (j d) -> p j d", j=NT)
        ln2 = head[:, NT * 2 * D:NT * 2 * D + 2 * D].rearrange("p (a d) -> p a d", a=2)

        ps = ctx.enter_context(nc.psum_tensor("ps", [P, 8, 512], F32))

        x_loaded = [sem(f"x_loaded{j}") for j in range(NT)]
        value_loaded = [sem(f"value_loaded{c}") for c in range(NG)]
        win_loaded = [sem(f"win_loaded{c}") for c in range(1, 4)]
        wout_loaded = [sem(f"wout_loaded{h}") for h in range(2)]
        rows_loaded = sem("rows_loaded")
        router_loaded = sem("router_loaded")
        ln1_loaded = sem("ln1_loaded")
        consts_made = sem("consts_made")
        fills_made = sem("fills_made")
        tile_padded = sem("tile_padded")
        x_turned = sem("x_turned")
        xT_high, xT_low = sem("xT_high"), sem("xT_low")
        w_high, w_low = sem("w_high"), sem("w_low")
        rows_turned = sem("rows_turned")
        rows_kept = sem("rows_kept")
        in_done = sem("in_done")
        in_act, in_dve = sem("in_act"), sem("in_dve")
        pooled_ready = sem("pooled_ready")
        map_done, map_kept = sem("map_done"), sem("map_kept")
        vtail_kept, utail_kept = sem("vtail_kept"), sem("utail_kept")
        mix_is_high, mix_is_low = sem("mix_is_high"), sem("mix_is_low")
        wout_is_high, wout_is_low = sem("wout_is_high"), sem("wout_is_low")
        tail_turned, tail_kept = sem("tail_turned"), sem("tail_kept")
        tail_stored = sem("tail_stored")
        out_done, out_kept = sem("out_done"), sem("out_kept")
        x1_ready, x1_stored = sem("x1_ready"), sem("x1_stored")
        var_ready, std_ready = sem("var_ready"), sem("std_ready")
        x1_turned = sem("x1_turned")
        x1T_ready = sem("x1T_ready")
        logits_done, logits_kept = sem("logits_done"), sem("logits_kept")
        diff_ready, exp_ready = sem("diff_ready"), sem("exp_ready")
        mask_ready = sem("mask_ready")
        pos_done, count_done = sem("pos_done"), sem("count_done")
        table_rhs_ready = sem("table_rhs_ready")
        table_done, table_ready = sem("table_done"), sem("table_ready")
        extra_ready = sem("extra_ready")
        w1_loaded = [sem(f"w1_loaded{u}") for u in range(RING)]
        w3_loaded = [sem(f"w3_loaded{u}") for u in range(RING)]
        w2_loaded = [sem(f"w2_loaded{u}") for u in range(RING)]
        matched, rel_moved = sem("matched"), sem("rel_moved")
        loads_due = sem("loads_due")
        hot_ready = sem("hot_ready")
        fetched, xe_kept = sem("fetched"), sem("xe_kept")
        xe_turned, xeT_ready = sem("xe_turned"), sem("xeT_ready")
        h1_done = sem("h1_done")
        h_done, silu_ready, h_ready = sem("h_done"), sem("silu_ready"), sem("h_ready")
        h_turned, hT_ready = sem("h_turned"), sem("hT_ready")
        y_done, ylo_kept, yhi_kept = sem("y_done"), sem("ylo_kept"), sem("yhi_kept")
        index_ready, issued = sem("index_ready"), sem("issued")
        scattered = sem("scattered")
        ln2_loaded = sem("ln2_loaded")
        total_loaded = [sem(f"total_loaded{j}") for j in range(NT)]
        bias_ready, centred = sem("bias_ready"), sem("centred")
        gained = sem("gained")
        dve_out, pool_out = sem("dve_out"), sem("pool_out")
        out_stored = sem("out_stored")
        step = sem("step")

        block = ctx.enter_context(nc.Block())

        def wait(eng, semaphore, value):
            if not (isinstance(value, int) and value == 0):
                eng.wait_ge(semaphore, value)

        turn_banks = [4, 5, 0, 1, 2, 3, 4, 5, 2, 3]

        def token_rows(tensor_prompt, tensor_sample, j):
            if j < NT - 1:
                return tensor_prompt[0, j * P:(j + 1) * P, :]
            return tensor_sample.rearrange("b s d -> (b s) d")

        @block.sync
        def _(sp):
            win = w_in.rearrange("(p k) c -> p k c", k=KD)
            wout = w_out.rearrange("(j p) d -> p j d", p=P)

            def load_x(j):
                sp.dma_start(x_tok[0:ROWS[j], j, :], token_rows(x_prompt, x_sample, j)).then_inc(x_loaded[j], 16)

            def load_values(c):
                sp.dma_start(win_a[:, :, c * P:(c + 1) * P], win[:, :, c * P:(c + 1) * P]).then_inc(value_loaded[c], 16)

            for j in range(3):
                load_x(j)
            load_values(0)
            for j in range(3, NT):
                load_x(j)
            for c in range(1, NG):
                load_values(c)
            sp.dma_start(pool_rows[0:NB * HIST, :], state_pool.rearrange("b h c -> (b h) c")).then_inc(rows_loaded, 16)
            sp.dma_start(conv_rows[0:NB * CHIST, :], state_conv.rearrange("b h c -> (b h) c")).then_inc(rows_loaded, 16)
            sp.dma_start(chan_rows[0:3, :], conv_w).then_inc(rows_loaded, 16)
            sp.dma_start(chan_rows[3:4, :], pool_scale.rearrange("(a c) -> a c", a=1)).then_inc(rows_loaded, 16)
            sp.dma_start(w_map[:, :, :], w_pool_map.rearrange("g c e -> c g e")).then_inc(rows_loaded, 16)
            sp.dma_start(win_b, win[:, :, 2 * DP:3 * DP]).then_inc(win_loaded[0], 16)
            sp.dma_start(w_router[:, :, 0:EG], w_group.rearrange("(p k) c -> p k c", k=KD)).then_inc(router_loaded, 16)
            sp.dma_start(w_router[:, :, EG:NR], w_expert.rearrange("(p k) c -> p k c", k=KD)).then_inc(router_loaded, 16)
            sp.dma_start(b_router[:, 0:EG], b_group.partition_broadcast(P)).then_inc(router_loaded, 16)
            sp.dma_start(b_router[:, EG:NR], b_expert.partition_broadcast(P)).then_inc(router_loaded, 16)
            sp.wait_ge(rows_kept, 2)
            sp.dma_start(ln1[:, 0, :], ln1_g.partition_broadcast(P)).then_inc(ln1_loaded, 16)
            sp.dma_start(ln1[:, 1, :], ln1_b.partition_broadcast(P)).then_inc(ln1_loaded, 16)

            def load_w1(u, e):
                load_in(w1_slot[u], w1, e, w1_loaded[u])

            def load_w3(u, e):
                load_in(w3_slot[u], w3, e, w3_loaded[u])

            def load_in(slot, w, e, loaded):
                src = w[e] if isinstance(e, int) else w[bass.DynSlice(e, 1)].rearrange("e d f -> (e d) f")
                sp.dma_start(slot.rearrange("p (g c) f -> p g c f", g=2),
                             src.rearrange("(g p c) f -> p g c f", g=2, c=KH)).then_inc(loaded, 16)

            def load_w2(u, e):
                sp.dma_start(w2_slot[u], expert_w2(e)).then_inc(w2_loaded[u], 16)

            def expert_w2(e):
                src = w2[e] if isinstance(e, int) else w2[bass.DynSlice(e, 1)].rearrange("e f d -> (e f) d")
                return src.rearrange("(k p) d -> p k d", p=P)

            sp.wait_ge(w_low, 4)
            sp.dma_start(win_a, win[:, :, 3 * DP:4 * DP]).then_inc(win_loaded[1], 16)
            sp.wait_ge(w_low, 8)
            sp.dma_start(win_b, win[:, :, DP:2 * DP]).then_inc(win_loaded[2], 16)
            sp.wait_ge(w_low, 12)
            sp.dma_start(win_a, wout[:, :, 0:512]).then_inc(wout_loaded[0], 16)
            sp.wait_ge(w_low, 16)
            sp.dma_start(win_b, wout[:, :, 512:D]).then_inc(wout_loaded[1], 16)
            sp.wait_ge(in_done, 16)
            load_w3(0, 0)
            load_w2(0, 0)
            sp.wait_ge(in_dve, 8)
            sp.wait_ge(utail_kept, NG)
            sp.wait_ge(tail_stored, 64)
            load_w2(1, 1)
            sp.wait_ge(out_done, NT)
            load_w2(2, 2)
            load_w1(2, 2)
            sp.wait_ge(out_done, 2 * NT)
            load_w1(0, 0)
            load_w1(1, 1)
            load_w3(1, 1)
            load_w3(2, 2)

            def load_tile(u, n, seq):
                b = (u - 1) % RING
                before, own = (n + 1) * 16 if u else n * 16, (n + 1) * 16
                sp.wait_ge(h1_done, seq - 2)
                sp.sem_inc(loads_due, 1)
                sp.wait_ge(w3_loaded[b], before)
                sp.sem_inc(loads_due, 1)
                load_w1(u, seq)
                sp.wait_ge(h_done, seq - 2)
                sp.sem_inc(loads_due, 1)
                sp.wait_ge(w2_loaded[b], before)
                sp.sem_inc(loads_due, 1)
                load_w3(u, seq)
                sp.wait_ge(y_done, seq - 2)
                sp.sem_inc(loads_due, 1)
                sp.wait_ge(w1_loaded[u], own)
                sp.sem_inc(loads_due, 1)
                load_w2(u, seq)

            with sp.Fori(1, E // RING) as n:
                for u in range(RING):
                    load_tile(u, n, n * RING + u)
            for e in range(E // RING * RING, E):
                load_tile(e % RING, e // RING, e)

            sp.wait_ge(extra_ready, 1)
            n_extra = sp.value_load(extra[0:1, XTILES:XTILES + 1], min_val=0, max_val=XTILES)
            with sp.If(n_extra > 0):
                sp.wait_ge(y_done, E - 2)
                e = sp.value_load(extra[0:1, 0:1], min_val=0, max_val=E - 1)
                load_w1(2, e)
                load_w3(2, e)
                load_w2(2, e)
            with sp.If(n_extra > 1):
                with sp.Fori(1, n_extra) as v:
                    sp.wait_ge(y_done, v + E)
                    e = sp.value_load(extra[0:1, bass.DynSlice(v, 1)], min_val=0, max_val=E - 1)
                    load_w1(2, e)
                    load_w3(2, e)
                    load_w2(2, e)

            sp.wait_ge(y_done, E - 1)
            sp.dma_start(ln2[:, 0, :], ln2_g.partition_broadcast(P)).then_inc(ln2_loaded, 16)
            sp.dma_start(ln2[:, 1, :], ln2_b.partition_broadcast(P)).then_inc(ln2_loaded, 16)
            sp.wait_ge(scattered, n_extra * 16 + 16 * E)
            for j in range(NT):
                r = ROWS[j]
                sp.dma_start(total[0:r, j], sums_dram[j * P:j * P + r]).then_inc(total_loaded[j], 16)
            for j in (0, 2, 1, 3, 4):
                if j < SHARED:
                    sp.wait_ge(pool_out, j + 1)
                else:
                    sp.wait_ge(dve_out, j - SHARED + 1)
                sp.dma_start(token_rows(y_prompt, y_sample, j), normed[0:ROWS[j], j, :]).then_inc(out_stored, 16)
            sp.wait_ge(out_stored, 16 * NT)

        @block.tensor
        def _(pe):
            x_view = x_tok[:, :, :].rearrange("p j (q k) -> p j k q", k=KD)

            pe.wait_ge(consts_made, 1)
            def turn_x(j):
                r = ROWS[j]
                pe.wait_ge(x_loaded[j], 16)
                for h in range(2):
                    if j >= 3:
                        pe.wait_ge(xT_low, (2, 6)[j - 3] + h - 1)
                    b = turn_banks[(2 * j + h) ]
                    for i in range(4):
                        mm = pe.transpose(ps[:, b, i * r:(i + 1) * r], x_view[0:r, j, 4 * h + i, :], ident[0:r, 0:r])
                    mm.then_inc(x_turned, 1)

            for j in range(4):
                turn_x(j)

            def turn_rows():
                pe.wait_ge(rows_loaded, 80)
                for g in range(NG):
                    mm = pe.transpose(ps[:, 6, g * 120:(g + 1) * 120], pool_rows[0:120, g * P:(g + 1) * P],
                                      ident[0:120, 0:120])
                mm.then_inc(rows_turned, 1)
                for g in range(NG):
                    pe.transpose(ps[:, 7, g * 4:(g + 1) * 4], chan_rows[0:4, g * P:(g + 1) * P], ident[0:4, 0:4])
                    mm = pe.transpose(ps[:, 7, 16 + g * 16:32 + g * 16], conv_rows[0:16, g * P:(g + 1) * P],
                                      ident[0:16, 0:16])
                mm.then_inc(rows_turned, 1)

            def project(c):
                part, g = c // NG, c % NG
                pe.wait_ge(w_low, c + 1)
                if c in (2, 3) or 4 <= c < 10:
                    pe.wait_ge(in_act, c - 1)
                elif c >= 10:
                    pe.wait_ge(in_dve, c - 9)
                for h in range(2):
                    if c == 0 and h:
                        turn_x(4)
                    if c == 0:
                        pe.wait_ge(xT_low, (6, 2 * NT)[h])
                    for i, (a, b) in enumerate(((0, 0), (0, 1), (1, 0))):
                        for k in range(KD):
                            mm = pe.matmul(ps[:, 2 * (c % 2) + h, 0:HALF], w_part[a][:, c % 2, k, :],
                                           xT[b][:, k, h * HALF:(h + 1) * HALF], start=(i == 0 and k == 0),
                                           stop=(i == 2 and k == KD - 1))
                mm.then_inc(in_done, 1)

            def pool_map(g):
                pe.wait_ge(pooled_ready, g + 1)
                if g:
                    pe.wait_ge(map_kept, g)
                else:
                    pe.wait_ge(rows_kept, 2)
                for h in range(2):
                    mm = pe.matmul(ps[:, 6 + h, 0:HALF], w_map[:, g, :], pooled[:, h * HALF:(h + 1) * HALF],
                                   start=True, stop=True)
                mm.then_inc(map_done, 1)

            def turn_tail(tail, n):
                for g in range(NG):
                    pe.transpose(ps[0:n, 4, g * P:(g + 1) * P], tail[:, g, 0:n], ident[:, :])
                    mm = pe.transpose(ps[0:NB * n, 5, g * P:(g + 1) * P], tail[:, g, n:n + NB * n], ident[:, :])
                mm.then_inc(tail_turned, 1)

            project(0)
            turn_rows()
            project(1)
            pool_map(0)
            project(2)
            pool_map(1)
            project(3)
            pool_map(2)
            project(4)
            pool_map(3)
            project(5)
            pe.wait_ge(vtail_kept, NG)
            turn_tail(vtail, HIST)
            for c in range(6, 13):
                project(c)
            pe.wait_ge(utail_kept, NG)
            pe.wait_ge(tail_kept, 1)
            turn_tail(utail, CHIST)
            for c in range(13, 16):
                project(c)

            def out_project(h, j):
                o = h * NT + j
                r = ROWS[j]
                if o == 0:
                    pe.wait_ge(in_dve, 7)
                elif o == 2:
                    pe.wait_ge(in_dve, 8)
                elif o >= 4:
                    pe.wait_ge(out_kept, o - 3)
                for k in range(KD):
                    if o == 0:
                        pe.wait_ge(mix_is_low, k + 1)
                    for i, (a, b) in enumerate(((0, 0), (0, 1), (1, 0))):
                        mm = pe.matmul(ps[0:r, o % 4, :], mix_part[a][:, k, j * P:j * P + r],
                                       wout_part[h][b][:, k, :], start=(i == 0 and k == 0),
                                       stop=(i == 2 and k == KD - 1))
                mm.then_inc(out_done, 1)

            def turn_x1(j):
                r = ROWS[j]
                pe.wait_ge(x1_ready, j + 1)
                if j:
                    pe.wait_ge(x1T_ready, 2 * j)
                else:
                    pe.wait_ge(tail_kept, 2)
                for k in range(KD):
                    mm = pe.transpose(ps[:, 4 + k // 4, (k % 4) * r:(k % 4 + 1) * r], x_view[0:r, j, k, :],
                                      ident[0:r, 0:r])
                    if k % 4 == 3:
                        mm.then_inc(x1_turned, 1)

            def route(j):
                r = ROWS[j]
                pe.wait_ge(x1T_ready, 2 * j + 2)
                if j >= 2:
                    pe.wait_ge(logits_kept, j - 1)
                for k in range(KD):
                    mm = pe.matmul(ps[0:r, 6 + j % 2, 0:NR], x1T[:, k, 0:r], w_router[:, k, :],
                                   start=(k == 0), stop=(k == KD - 1))
                mm.then_inc(logits_done, 1)

            pe.wait_ge(wout_is_low, 1)
            for j in range(NT):
                out_project(0, j)
            pe.wait_ge(wout_is_low, 2)
            pe.wait_ge(router_loaded, 64)
            out_project(1, 0)
            out_project(1, 1)
            turn_x1(0)
            for j in range(2, NT):
                out_project(1, j)
                route(j - 2)
                turn_x1(j - 1)
            for j in range(NT - 2, NT):
                route(j)
                if j + 1 < NT:
                    turn_x1(j + 1)

            def keep_warm(products):
                for _ in range(products):
                    pe.matmul(ps[:, 0, 0:P], ident[:, :], ident[:, :], start=True, stop=True)

            keep_warm(21)
            pe.wait_ge(mask_ready, 1)
            for i in range(NT):
                for j in range(i + 1):
                    mm = pe.matmul(ps[:, 5, i * E:(i + 1) * E], before[:, :] if j == i else ones[:, :], mask[:, j, :],
                                   start=(j == 0), stop=(j == i))
            mm.then_inc(pos_done, 1)
            for j in range(NT):
                mm = pe.matmul(ps[:, 6, 0:E], ones[:, :], mask[:, j, :], start=(j == 0), stop=(j == NT - 1))
            mm.then_inc(count_done, 1)

            def fetch(seq, i, before_last=None):
                pe.wait_ge(hot_ready, seq + 1)
                for j in range(NT):
                    if before_last and j == NT - 1:
                        before_last()
                    for g in range(2):
                        mm = pe.matmul(ps[64 * g:64 * g + 64, BX, :], hot[i][:, j, :], x_tok[:, j, g * DH:(g + 1) * DH],
                                       start=(j == 0), stop=(j == NT - 1))
                mm.then_inc(fetched, 1)

            def turn_tile(seq):
                pe.wait_ge(xe_kept, seq + 1)
                v = xe.rearrange("p (q c) -> p c q", c=KH)
                for c in range(KH):
                    mm = pe.transpose(ps[:, BXT, c * P:(c + 1) * P], v[:, c, :], ident[:, :])
                mm.then_inc(xe_turned, 1)

            def hidden(u, n, seq, in_between=None):
                pe.wait_ge(xeT_ready, seq + 1)
                for w, loaded, done, b in ((w1_slot[u], w1_loaded[u], h1_done, B1), (w3_slot[u], w3_loaded[u], h_done, B3)):
                    pe.wait_ge(loaded, n * 16 + 16)
                    for k in range(KD):
                        x = xeT[:, k % KH, k // KH * SLOTS:(k // KH + 1) * SLOTS]
                        for g in range(2):
                            mm = pe.matmul(ps[64 * g:64 * g + 64, b, 0:FH], x, w[:, k, g * FH:(g + 1) * FH],
                                           start=(k == 0), stop=(k == KD - 1))
                    mm.then_inc(done, 1)
                    if in_between and done is h1_done:
                        in_between()

            def turn_hidden(seq):
                pe.wait_ge(h_ready, seq + 1)
                for c in range(2):
                    mm = pe.transpose(ps[:, BHT, c * P:(c + 1) * P], h_rows[:, c * P:(c + 1) * P], ident[:, :])
                mm.then_inc(h_turned, 1)

            def down(u, n, seq, halfway=None):
                pe.wait_ge(w2_loaded[u], n * 16 + 16)
                wait(pe, ylo_kept, seq)
                wait(pe, yhi_kept, seq)
                pe.wait_ge(hT_ready, seq + 1)
                for k in range(KF):
                    if halfway and k == KF // 2:
                        halfway()
                    for g in range(2):
                        mm = pe.matmul(ps[64 * g:64 * g + 64, BY, :], hT[:, k % 2, k // 2 * SLOTS:(k // 2 + 1) * SLOTS],
                                       w2_slot[u][:, k, g * DH:(g + 1) * DH], start=(k == 0), stop=(k == KF - 1))
                mm.then_inc(y_done, 1)

            def tile(u, n, seq, following, in_between=None):
                hidden(u, n, seq, in_between)
                if following is None:
                    turn_hidden(seq)
                    down(u, n, seq)
                else:
                    fetch(seq + 1, following, lambda: turn_hidden(seq))
                    down(u, n, seq, lambda: turn_tile(seq + 1))

            def token_table():
                pe.wait_ge(table_rhs_ready, 1)
                for a in range(2 * NT):
                    for g in range(2):
                        mm = pe.matmul(ps[64 * g:64 * g + 64, 7, 0:2 * TILES], hot_col[:, a, :],
                                       slot_val[:, a, :, :].rearrange("p b c -> p (b c)"), start=(a == 0),
                                       stop=(a == 2 * NT - 1))
                mm.then_inc(table_done, 1)

            keep_warm(12)
            fetch(0, 0)
            turn_tile(0)
            tile(0, 0, 0, 1, token_table)
            tile(1, 0, 1, 2)
            tile(2, 0, 2, 0)
            with pe.Fori(1, E // RING) as n:
                for u in range(RING):
                    tile(u, n, n * RING + u, (u + 1) % RING)
            tile(0, E // RING, E - 2, 1)
            tile(1, E // RING, E - 1, None)

            pe.wait_ge(extra_ready, 1)
            n_extra = pe.value_load(extra[0:1, XTILES:XTILES + 1], min_val=0, max_val=XTILES)
            with pe.If(n_extra > 0):
                with pe.Fori(0, n_extra) as v:
                    fetch(v + E, 2)
                    turn_tile(v + E)
                    tile(2, v + E // RING, v + E, None)

        @block.scalar
        def _(act):
            def copy(out, in_, **kw):
                return nc.scalar.activation(out, in_, ACT.Copy, **kw)

            def high_of_x(i):
                j, h = i // 2, i % 2
                r = ROWS[j]
                act.wait_ge(x_turned, i + 1)
                copy(xT[0][:, 4 * h:4 * h + 4, j * P:j * P + r],
                     ps[:, turn_banks[i], 0:4 * r].rearrange("p (k t) -> p k t", k=4)).then_inc(xT_high, 1)

            def high_of_w(c):
                part, g = c // NG, c % NG
                if part == 0:
                    act.wait_ge(value_loaded[g], 16)
                elif g == 0:
                    act.wait_ge(win_loaded[part - 1], 16)
                if c >= 2:
                    act.wait_ge(in_done, c - 1)
                copy(w_part[0][:, c % 2, :, :], (win_a, win_b)[part % 2][:, :, g * P:(g + 1) * P]).then_inc(w_high, 1)

            for i in range(6):
                high_of_x(i)
            high_of_w(0)
            for i in range(6, 2 * NT):
                high_of_x(i)
            high_of_w(1)

            def keep_values(g):
                act.wait_ge(in_done, g + 1)
                if g >= 2:
                    act.wait_ge(pooled_ready, g - 1)
                    act.wait_ge(vtail_kept, g - 1)
                b = 2 * (g % 2)
                v = vext[g % 2]
                copy(v[:, HIST:HIST + HALF], ps[:, b, 0:HALF])
                copy(v[:, HIST + HALF:PV], ps[:, b + 1, 0:SEQ - HALF])
                copy(v[:, PV:VEXT].rearrange("p (b t) -> p b t", b=NB)[:, :, HIST:],
                     ps[:, b + 1, SEQ - HALF:HALF].rearrange("p (b t) -> p b t", b=NB)).then_inc(in_act, 1)

            def keep_map(g):
                act.wait_ge(map_done, g + 1)
                nc.scalar.activation(mixT[:, g, 0:HALF], ps[:, 6, 0:HALF], ACT.Identity, scale=chan[:, g, 3:4])
                nc.scalar.activation(mixT[:, g, HALF:T], ps[:, 7, 0:HALF], ACT.Identity,
                                     scale=chan[:, g, 3:4]).then_inc(map_kept, 1)

            def keep_c(g):
                act.wait_ge(in_done, NG + g + 1)
                b = 2 * (g % 2)
                copy(mixT[:, NG + g, 0:HALF], ps[:, b, 0:HALF])
                copy(mixT[:, NG + g, HALF:T], ps[:, b + 1, 0:HALF]).then_inc(in_act, 1)

            keep_values(0)
            high_of_w(2)
            keep_values(1)
            high_of_w(3)
            keep_map(0)
            keep_values(2)
            high_of_w(4)
            keep_map(1)
            keep_values(3)
            high_of_w(5)
            keep_map(2)
            keep_c(0)
            high_of_w(6)
            keep_map(3)
            keep_c(1)
            high_of_w(7)
            act.wait_ge(pooled_ready, NG)
            act.wait_ge(tail_turned, 1)
            copy(wsum[0][0:HIST, 0:DP], ps[0:HIST, 4, :])
            copy(wsum[1][0:NB * HIST, 0:DP], ps[0:NB * HIST, 5, :]).then_inc(tail_kept, 1)
            act.wait_ge(tail_kept, 1)
            act.dma_start(pool_prompt[0], wsum[0][0:HIST, 0:DP]).then_inc(tail_stored, 16)
            act.dma_start(pool_sample.rearrange("b h c -> (b h) c"), wsum[1][0:NB * HIST, 0:DP]).then_inc(tail_stored, 16)
            keep_c(2)
            high_of_w(8)
            keep_c(3)

            def high_of_mix(k):
                if k < NG:
                    act.wait_ge(map_kept, k + 1)
                else:
                    act.wait_ge(in_dve, k + 1)
                copy(mix_high[:, k, :], mixT[:, k, :]).then_inc(mix_is_high, 1)

            def high_of_wout(h):
                act.wait_ge(wout_loaded[h], 16)
                if h:
                    act.wait_ge(in_done, 16)
                copy(wout_part[h][0][:, :, :], (win_a, win_b)[h]).then_inc(wout_is_high, 1)

            for k in range(NG):
                high_of_mix(k)
            for c in range(9, 14):
                high_of_w(c)
            high_of_mix(4)
            high_of_w(14)
            high_of_mix(5)
            high_of_w(15)
            high_of_wout(0)
            high_of_mix(6)
            act.wait_ge(tail_turned, 2)
            copy(pooled[0:CHIST, 0:DP], ps[0:CHIST, 4, :])
            copy(equal_flat[0:NB * CHIST, 0:DP], ps[0:NB * CHIST, 5, :]).then_inc(tail_kept, 1)
            act.wait_ge(tail_kept, 2)
            act.dma_start(conv_prompt[0], pooled[0:CHIST, 0:DP]).then_inc(tail_stored, 16)
            act.dma_start(conv_sample.rearrange("b h c -> (b h) c"), equal_flat[0:NB * CHIST, 0:DP]).then_inc(tail_stored, 16)

            high_of_mix(7)
            high_of_wout(1)

            def keep_x1T(j):
                r = ROWS[j]
                for h in range(2):
                    act.wait_ge(x1_turned, 2 * j + h + 1)
                    if j:
                        act.wait_ge(logits_done, j)
                    copy(x1T[:, 4 * h:4 * h + 4, 0:r],
                         ps[:, 4 + h, 0:4 * r].rearrange("p (k t) -> p k t", k=4)).then_inc(x1T_ready, 1)

            def deviation(n, r, eps_):
                act.wait_ge(var_ready, n + 1)
                nc.scalar.activation(std[0:r, :], mv[0:r, 1:2], ACT.Sqrt, bias=eps_[0:r, :]).then_inc(std_ready, 1)

            act.wait_ge(consts_made, 2)
            act.wait_ge(tile_padded, 1)
            deviation(0, P, eps[:, 0:1])
            for j in range(NT):
                if j + 1 < NT:
                    deviation(j + 1, ROWS[j + 1], eps[:, 0:1])
                act.wait_ge(x1_ready, j + 1)
                act.dma_start(sums_dram[j * P:(j + 1) * P, :], x_tok[:, j, :]).then_inc(x1_stored, 16)
                keep_x1T(j)
            act.wait_ge(diff_ready, 1)
            nc.scalar.activation(g_exp, g_tmp, ACT.Exp).then_inc(exp_ready, 1)
            act.wait_ge(diff_ready, 2)
            nc.scalar.activation(top[:, 3, :], top[:, 2, :], ACT.Exp).then_inc(exp_ready, 1)

            def silu_of(seq):
                act.wait_ge(h1_done, seq + 1)
                nc.scalar.activation(silu, ps[:, B1, 0:FH], ACT.Silu).then_inc(silu_ready, 1)

            def keep_xe(seq):
                act.wait_ge(fetched, seq + 1)
                copy(xe, ps[:, BX, :]).then_inc(xe_kept, 1)

            def keep_xeT(seq):
                act.wait_ge(xe_turned, seq + 1)
                copy(xeT, ps[:, BXT, :].rearrange("p (c s) -> p c s", c=KH)).then_inc(xeT_ready, 1)

            def keep_y(u, seq, left):
                wait(act, scattered, left * 16)
                act.wait_ge(y_done, seq + 1)
                copy(ye[u][0:SLOTS, 0:DH], ps[0:SLOTS, BY, :]).then_inc(ylo_kept, 1)

            def tile(u, seq, left):
                silu_of(seq)
                keep_xe(seq + 1)
                keep_xeT(seq + 1)
                keep_y(u, seq, left)

            keep_xe(0)
            keep_xeT(0)
            for seq in range(RING):
                tile(seq, seq, 0)
            with act.Fori(1, E // RING) as n:
                for u in range(RING):
                    tile(u, n * RING + u, n * RING + (u - 2))
            tile(0, E - 2, E - 4)
            silu_of(E - 1)
            keep_y(1, E - 1, E - 3)

            act.wait_ge(extra_ready, 1)
            n_extra = act.value_load(extra[0:1, XTILES:XTILES + 1], min_val=0, max_val=XTILES)
            with act.If(n_extra > 0):
                with act.Fori(0, n_extra) as v:
                    keep_xe(v + E)
                    keep_xeT(v + E)
                    silu_of(v + E)
                    keep_y(2, v + E, v + E)

            for j in range(NT):
                r = ROWS[j]
                deviation(NT + j, r, eps[:, 1:2])
                if j < SHARED:
                    act.wait_ge(bias_ready, j + 1)
                    nc.scalar.activation(normed[0:r, j, :], total[0:r, j, :], ACT.Identity, bias=rstd[0:r, j, 1:2],
                                         scale=rstd[0:r, j, 0:1]).then_inc(centred, 1)

        @block.gpsimd
        def _(pool):
            g = nc.gpsimd
            g.memset(ident[:, :], 0.0).then_inc(fills_made, 1)
            g.memset(before[:, :], 1.0).then_inc(fills_made, 1)
            pool.wait_ge(fills_made, 2)
            g.affine_select(out=ident[:, :], in_=ident[:, :], compare_op=ALU.not_equal, fill=1.0, base=0,
                            pattern=[[-1, P]], channel_multiplier=1).then_inc(consts_made, 1)
            g.affine_select(out=before[:, :], in_=before[:, :], compare_op=ALU.is_gt, fill=0.0, base=0,
                            pattern=[[1, P]], channel_multiplier=-1)
            for i in range(2):
                g.memset(vext[i][:, 0:HIST], 0.0)
            g.iota(counts, [[1, HIST]], base=1, channel_multiplier=0,
                   allow_small_or_imprecise_dtypes=True).then_inc(fills_made, 1)
            g.memset(ones[:, :], 1.0)
            g.memset(eps[:, 0:1], EPS)
            g.memset(eps[:, 1:2], EPS / ALPHA ** 2)
            g.memset(logits[:, NT - 1, :], 0.0)
            g.iota(iota[:, :], [[1, SLOTS]], base=0, channel_multiplier=0, allow_small_or_imprecise_dtypes=True)
            g.iota(rev[:, :], [[-1, EPG]], base=EPG, channel_multiplier=0, allow_small_or_imprecise_dtypes=True)
            g.iota(edges[:, :], [[SLOTS, NQ]], base=SLOTS, channel_multiplier=0, allow_small_or_imprecise_dtypes=True)
            g.iota(pad_row[:, :], [[0, 1]], base=T + 1, channel_multiplier=1, allow_small_or_imprecise_dtypes=True)
            g.iota(tokval[:, :], [[P, NT]], base=1, channel_multiplier=1,
                   allow_small_or_imprecise_dtypes=True).then_inc(fills_made, 1)
            pool.wait_ge(fills_made, 4)
            g.memset(tokval[64:P, NT - 1:NT], 0.0).then_inc(consts_made, 1)
            pool.wait_ge(consts_made, 2)

            for c in range(NG):
                v = vext[c % 2]
                pool.wait_ge(in_act, c + 1)
                g.tensor_copy(vtail[:, c, 0:HIST], v[:, PV - HIST:PV])
                pool.wait_ge(pooled_ready, c + 1)
                g.tensor_copy(vtail[:, c, HIST:VTAIL].rearrange("p (b t) -> p b t", b=NB),
                              v[:, PV:VEXT].rearrange("p (b t) -> p b t", b=NB)[:, :, NS:]).then_inc(vtail_kept, 1)
            for c in range(NG):
                pool.wait_ge(in_dve, c + 1)
                v = vext[c % 2]
                g.tensor_copy(utail[:, c, 0:CHIST], v[:, PU - CHIST:PU])
                g.tensor_copy(utail[:, c, CHIST:UTAIL].rearrange("p (b t) -> p b t", b=NB),
                              v[:, PU:UEXT].rearrange("p (b t) -> p b t", b=NB)[:, :, NS:]).then_inc(utail_kept, 1)
            def add_outputs(u, seq):
                wait(pool, scattered, seq * 16)
                g.tensor_copy(scatter_idx[0:SLOTS, :],
                              slot_row[0:SLOTS, bass.DynSlice(seq, 1)]).then_inc(index_ready, 1)
                pool.wait_ge(index_ready, seq + 1)
                pool.wait_ge(ylo_kept, seq + 1)
                pool.wait_ge(yhi_kept, seq + 1)
                pool.sem_inc(issued, 1)
                g.indirect_dma_start(out=sums_dram[:, :],
                                     out_offset=bass.IndirectOffsetOnAxis(ap=scatter_idx[0:SLOTS, 0:1], axis=0),
                                     in_=ye[u][0:SLOTS, :], in_offset=None, bounds_check=last_row,
                                     oob_is_err=True, compute_op=ALU.add).then_inc(scattered, 16)

            last_row = pool.to_reg(T + SLOTS - 1)
            pool.wait_ge(table_ready, 1)
            pool.wait_ge(x1_stored, 16 * NT)
            for seq in range(RING):
                add_outputs(seq, seq)
            with pool.Fori(1, E // RING) as n:
                for u in range(RING):
                    add_outputs(u, n * RING + u)
            add_outputs(0, E - 2)
            add_outputs(1, E - 1)

            pool.wait_ge(extra_ready, 1)
            n_extra = pool.value_load(extra[0:1, XTILES:XTILES + 1], min_val=0, max_val=XTILES)
            with pool.If(n_extra > 0):
                with pool.Fori(0, n_extra) as v:
                    add_outputs(2, v + E)

            pool.wait_ge(ln2_loaded, 32)
            for j in range(SHARED):
                row = normed[0:ROWS[j], j, :]
                pool.wait_ge(centred, j + 1)
                g.tensor_tensor(row, row, ln2[0:ROWS[j], 0, :], ALU.mult).then_inc(gained, 1)
                pool.wait_ge(gained, j + 1)
                g.tensor_tensor(row, row, ln2[0:ROWS[j], 1, :], ALU.add).then_inc(pool_out, 1)

        @block.vector
        def _(dve):
            v = nc.vector
            steps = [0]
            deviations = [0]

            def settled(ins):
                steps[0] += 1
                ins.then_inc(step, 1)
                dve.wait_ge(step, steps[0])

            v.memset(x_tok[ROWS[NT - 1]:P, NT - 1, :], 0.0).then_inc(tile_padded, 1)
            def low_of_x(i):
                j, h = i // 2, i % 2
                r = ROWS[j]
                high, low = [x[:, 4 * h:4 * h + 4, j * P:j * P + r] for x in xT]
                dve.wait_ge(xT_high, i + 1)
                v.tensor_tensor(low, ps[:, turn_banks[i], 0:4 * r].rearrange("p (k t) -> p k t", k=4), high,
                                ALU.subtract).then_inc(xT_low, 1)

            def low_of_w(c):
                high, low = [w[:, c % 2, :, :] for w in w_part]
                g = c % NG
                dve.wait_ge(w_high, c + 1)
                v.tensor_tensor(low, (win_a, win_b)[c // NG % 2][:, :, g * P:(g + 1) * P], high,
                                ALU.subtract).then_inc(w_low, 1)

            for i in range(6):
                low_of_x(i)
            low_of_w(0)
            for i in range(6, 2 * NT):
                low_of_x(i)
            low_of_w(1)
            dve.wait_ge(rows_turned, 1)
            v.tensor_copy(poolT, ps[:, 6, 0:480].rearrange("p (j t) -> p j t", j=NG)).then_inc(rows_kept, 1)
            dve.wait_ge(rows_turned, 2)
            v.tensor_copy(chan[:, :, :], ps[:, 7, 0:16].rearrange("p (j t) -> p j t", j=NG))
            v.tensor_copy(convT, ps[:, 7, 16:80].rearrange("p (j t) -> p j t", j=NG)).then_inc(rows_kept, 1)
            dve.wait_ge(rows_kept, 2)
            dve.wait_ge(fills_made, 3)
            settled(v.reciprocal(counts, counts))

            for c in range(NG):
                w = 2 << c
                val = vext[c % 2]
                sample = val[:, PV:VEXT].rearrange("p (b t) -> p b t", b=NB)
                low_of_w(c + 2)
                if c >= 2:
                    dve.wait_ge(vtail_kept, c - 1)
                settled(v.tensor_copy(sample[:, :, 0:HIST], poolT[:, c, :].rearrange("p (b t) -> p b t", b=NB)))
                dve.wait_ge(in_act, c + 1)
                src, reach = val, 1
                for s in range(c + 1):
                    dst = wsum[s % 2]
                    lo = 2 * reach - 1
                    settled(v.tensor_tensor(dst[:, lo:VEXT], src[:, lo:VEXT], src[:, lo - reach:VEXT - reach], ALU.add))
                    src, reach = dst, 2 * reach
                if c:
                    dve.wait_ge(map_done, c)
                ssum = src[:, PV:VEXT].rearrange("p (b t) -> p b t", b=NB)
                v.scalar_tensor_tensor(pooled[:, w - 1:SEQ], src[:, HIST + w - 1:PV], 1.0 / w,
                                       val[:, HIST + w - 1:PV], ALU.mult, ALU.subtract)
                v.scalar_tensor_tensor(pooled[:, SEQ:T].rearrange("p (b t) -> p b t", b=NB), ssum[:, :, HIST:], 1.0 / w,
                                       sample[:, :, HIST:], ALU.mult, ALU.subtract)
                settled(v.tensor_tensor(pooled[:, 0:w - 1], src[:, HIST:HIST + w - 1], counts[:, 0:w - 1], ALU.mult))
                v.tensor_tensor(pooled[:, 0:w - 1], pooled[:, 0:w - 1], val[:, HIST:HIST + w - 1],
                                ALU.subtract).then_inc(pooled_ready, 1)

            def low_of_mix(k):
                dve.wait_ge(mix_is_high, k + 1)
                v.tensor_tensor(mix_low[:, k, :], mixT[:, k, :], mix_high[:, k, :], ALU.subtract).then_inc(mix_is_low, 1)

            def low_of_wout(h):
                dve.wait_ge(wout_is_high, h + 1)
                v.tensor_tensor(wout_part[h][1][:, :, :], (win_a, win_b)[h], wout_part[h][0][:, :, :],
                                ALU.subtract).then_inc(wout_is_low, 1)

            for c in range(6, 9):
                low_of_w(c)
            for c in range(NG):
                low_of_w(c + 9)
                b = 2 * (c % 2)
                u = vext[c % 2]
                us = u[:, PU:UEXT].rearrange("p (b t) -> p b t", b=NB)
                gate = mixT[:, NG + c, :]
                if c < 2:
                    dve.wait_ge(vtail_kept, NG)
                else:
                    dve.wait_ge(utail_kept, c - 1)
                v.tensor_copy(us[:, :, 0:CHIST], convT[:, c, :].rearrange("p (b t) -> p b t", b=NB))
                dve.wait_ge(in_act, NG + c + 1)
                dve.wait_ge(in_done, 2 * NG + c + 1)
                v.tensor_tensor(u[:, CHIST:CHIST + HALF], gate[:, 0:HALF], ps[:, b, 0:HALF], ALU.mult)
                v.tensor_tensor(u[:, CHIST + HALF:PU], gate[:, HALF:SEQ], ps[:, b + 1, 0:SEQ - HALF], ALU.mult)
                settled(v.tensor_tensor(us[:, :, CHIST:], gate[:, SEQ:T].rearrange("p (b t) -> p b t", b=NB),
                                        ps[:, b + 1, SEQ - HALF:HALF].rearrange("p (b t) -> p b t", b=NB), ALU.mult))
                dve.sem_inc(in_dve, 1)
                gp, gs = gate[:, 0:SEQ], gate[:, SEQ:T].rearrange("p (b t) -> p b t", b=NB)
                v.tensor_scalar(gp, u[:, 0:SEQ], chan[:, c, 0:1], None, ALU.mult)
                settled(v.tensor_scalar(gs, us[:, :, 0:NS], chan[:, c, 0:1], None, ALU.mult))
                for k in (1, 2):
                    v.scalar_tensor_tensor(gp, u[:, k:SEQ + k], chan[:, c, k:k + 1], gp, ALU.mult, ALU.add)
                    settled(v.scalar_tensor_tensor(gs, us[:, :, k:NS + k], chan[:, c, k:k + 1], gs, ALU.mult, ALU.add))
                low_of_mix(c)

            for c in range(NG):
                if c + 13 < 4 * NG:
                    low_of_w(c + 13)
                if c == 2:
                    low_of_wout(0)
                b = 2 * (c % 2)
                dve.wait_ge(in_done, 3 * NG + c + 1)
                v.tensor_tensor(mixT[:, NG + c, 0:HALF], mixT[:, NG + c, 0:HALF], ps[:, b, 0:HALF], ALU.mult)
                v.tensor_tensor(mixT[:, NG + c, HALF:T], mixT[:, NG + c, HALF:T], ps[:, b + 1, 0:HALF],
                                ALU.mult).then_inc(in_dve, 1)
                low_of_mix(NG + c)
            low_of_wout(1)

            def residual(h, j):
                o, r = h * NT + j, ROWS[j]
                dve.wait_ge(out_done, o + 1)
                x = x_tok[0:r, j, h * 512:(h + 1) * 512]
                return v.scalar_tensor_tensor(x, x, ALPHA, ps[0:r, o % 4, :], ALU.mult, ALU.add)

            def deviation_of(row, r):
                v.bn_stats(stats[0:r, 0, :], row[:, 0:512])
                settled(v.bn_stats(stats[0:r, 1, :], row[:, 512:D]))
                settled(v.bn_aggr(mv[0:r, :], stats[0:r, :, :].rearrange("p a b -> p (a b)")))
                dve.sem_inc(var_ready, 1)

            def scale_of(r, scale):
                deviations[0] += 1
                dve.wait_ge(std_ready, deviations[0])
                settled(v.reciprocal(scale, std[0:r, :]))

            def norm1(j):
                r = ROWS[j]
                settled(residual(1, j))
                dve.sem_inc(out_kept, 1)
                row = x_tok[0:r, j, :]
                deviation_of(row, r)
                v.scalar_tensor_tensor(row, row, mv[0:r, 0:1], ln1[0:r, 0, :], ALU.subtract, ALU.mult)
                scale_of(r, rstd[0:r, j, 0:1])
                v.scalar_tensor_tensor(row, row, rstd[0:r, j, 0:1], ln1[0:r, 1, :], ALU.mult,
                                       ALU.add).then_inc(x1_ready, 1)

            def keep_logits(j):
                r = ROWS[j]
                dve.wait_ge(logits_done, j + 1)
                v.tensor_tensor(logits[0:r, j, :], ps[0:r, 6 + j % 2, 0:NR], b_router[0:r, :], ALU.add).then_inc(logits_kept, 1)

            for j in range(NT):
                residual(0, j).then_inc(out_kept, 1)
            dve.wait_ge(ln1_loaded, 32)
            dve.wait_ge(router_loaded, 64)
            dve.wait_ge(consts_made, 2)
            for j in range(4):
                norm1(j)
            keep_logits(0)
            keep_logits(1)
            norm1(4)
            for j in range(2, NT):
                keep_logits(j)
            dve.wait_ge(logits_kept, NT)

            def choose(n_, src, largest, hot, tmp):
                wide = [P, NT, n_]
                settled(v.tensor_reduce(largest, src, AX.X, ALU.max))
                settled(v.tensor_tensor(tmp, src, largest.unsqueeze(2).to_broadcast(wide), ALU.is_equal))
                settled(v.tensor_tensor(tmp, tmp, rev[:, 0:n_].unsqueeze(1).to_broadcast(wide), ALU.mult))
                settled(v.tensor_reduce(best, tmp, AX.X, ALU.max))
                settled(v.tensor_tensor(hot, tmp, best.unsqueeze(2).to_broadcast(wide), ALU.is_equal))

            lg = logits[:, :, 0:EG]
            le = logits[:, :, EG:NR].rearrange("p n (g e) -> p n g e", g=EG)
            gmax, m1, m2, ex = [top[:, i, :] for i in range(4)]
            choose(EG, lg, gmax, g_hot, g_tmp)
            v.tensor_tensor(g_tmp, lg, gmax.unsqueeze(2).to_broadcast([P, NT, EG]), ALU.subtract).then_inc(diff_ready, 1)
            lsel = in_group.rearrange("p n (g e) -> p n g e", g=EG)
            settled(v.tensor_tensor(lsel, le, g_hot.unsqueeze(3).to_broadcast([P, NT, EG, EPG]), ALU.mult))
            settled(v.tensor_reduce(e_val, lsel.rearrange("p n g e -> p n e g"), AX.X, ALU.add))
            choose(EPG, e_val, m1, e_hot[:, :, 0, :], e_tmp)
            settled(v.scalar_tensor_tensor(e_val, e_hot[:, :, 0, :], -3.0e38, e_val, ALU.mult, ALU.add))
            choose(EPG, e_val, m2, e_hot[:, :, 1, :], e_tmp)
            v.tensor_tensor(m2, m2, m1, ALU.subtract).then_inc(diff_ready, 1)
            for k in range(2):
                last = v.tensor_tensor(picked[:, :, k, :].rearrange("p n (g e) -> p n g e", g=EG),
                                       g_hot.unsqueeze(3).to_broadcast([P, NT, EG, EPG]),
                                       e_hot[:, :, k, :].unsqueeze(2).to_broadcast([P, NT, EG, EPG]), ALU.mult)
            settled(last)
            settled(v.memset(picked[64:P, NT - 1, :, :], 0.0))
            v.tensor_tensor(mask, picked[:, :, 0, :], picked[:, :, 1, :], ALU.add).then_inc(mask_ready, 1)

            pick = picked.rearrange("p n k e -> p (n k) e")
            prod = product.rearrange("p n k e -> p (n k) e")
            A = 2 * NT

            def row(x, n):
                return x.unsqueeze(1).to_broadcast([P, n, x.shape[-1]])

            settled(v.tensor_tensor(prod, pick, row(iota[:, 0:E], A), ALU.mult))
            settled(v.tensor_reduce(expert, prod, AX.X, ALU.add))
            dve.wait_ge(tail_stored, 64)
            dve.wait_ge(pos_done, 1)
            settled(v.tensor_tensor(product, picked, ps[:, 5, 0:NT * E].rearrange("p (n e) -> p n e", n=NT)
                                    .unsqueeze(2).to_broadcast([P, NT, 2, E]), ALU.mult))
            settled(v.tensor_reduce(pos, prod, AX.X, ALU.add))
            settled(v.tensor_scalar(col, pos, float(SLOTS), 1.0e6, ALU.is_ge, ALU.mult))
            settled(v.scalar_tensor_tensor(base, expert, float(SLOTS), pos, ALU.mult, ALU.add))
            settled(v.tensor_tensor(rel[:, :], base, col, ALU.add))

            def match_slots(seq, used):
                wait(dve, fetched, used)
                wait(dve, hot_ready, seq)
                wait(dve, rel_moved, seq)
                v.tensor_tensor(equal[:, :, :], iota[:, :].unsqueeze(1).to_broadcast([P, A, SLOTS]),
                                rel[:, :].unsqueeze(2).to_broadcast([P, A, SLOTS]), ALU.is_equal).then_inc(matched, 1)

            def sum_choices(seq, i):
                dve.wait_ge(matched, seq + 1)
                both = equal[:, :, :].rearrange("p (n k) c -> p n k c", k=2)
                v.tensor_tensor(hot[i], both[:, :, 0, :], both[:, :, 1, :], ALU.add).then_inc(hot_ready, 1)

            def move_rel(seq):
                dve.wait_ge(matched, seq + 1)
                v.tensor_scalar(rel[:, :], rel[:, :], -float(SLOTS), None, ALU.add).then_inc(rel_moved, 1)

            def make_hot(seq, i, used):
                match_slots(seq, used)
                move_rel(seq)
                sum_choices(seq, i)

            make_hot(0, 0, 0)
            match_slots(1, 0)
            sum_choices(1, 1)

            dve.wait_ge(exp_ready, 2)
            settled(v.tensor_reduce(best, g_exp, AX.X, ALU.add))
            settled(v.tensor_scalar(lift, ex, 1.0, ALPHA, ALU.add, ALU.mult))
            settled(v.tensor_tensor(lift, lift, best, ALU.mult))
            settled(v.reciprocal(gates[:, :, 0], lift))
            settled(v.tensor_tensor(gates[:, :, 1], gates[:, :, 0], ex, ALU.mult))
            settled(v.memset(gates[64:P, NT - 1, :], 0.0))

            dve.wait_ge(count_done, 1)
            settled(v.tensor_copy(cnt, ps[:, 6, 0:E]))
            settled(v.tensor_tensor(past_cnt, cnt.unsqueeze(2).to_broadcast([P, E, NQ]), row(edges[:, :], E), ALU.is_gt))
            settled(v.tensor_reduce(further, past_cnt, AX.X, ALU.add))
            settled(v.tensor_tensor_scan(upto, ones[:, 0:E], further, 0.0, ALU.mult, ALU.add))
            settled(v.tensor_tensor(first, upto, further, ALU.subtract))
            settled(v.tensor_tensor(prod, pick, row(first, A), ALU.mult))
            settled(v.tensor_reduce(base, prod, AX.X, ALU.add))
            settled(v.tensor_tensor(past_pos, pos.unsqueeze(2).to_broadcast([P, A, NQ]), row(edges[:, :], A), ALU.is_ge))
            settled(v.tensor_reduce(quot, past_pos, AX.X, ALU.add))
            settled(v.scalar_tensor_tensor(col, quot, -float(SLOTS), pos, ALU.mult, ALU.add))
            settled(v.tensor_tensor(base, base, quot, ALU.add))
            settled(v.tensor_tensor(base, base, expert, ALU.subtract))
            settled(v.tensor_scalar(base, base, float(E - 1), None, ALU.add))
            settled(v.scalar_tensor_tensor(tile_no, quot, 0.0, base, ALU.is_gt, ALU.mult))
            settled(v.tensor_tensor(tile_no, tile_no, expert, ALU.add))
            settled(v.scalar_tensor_tensor(rel[:, :], tile_no, float(SLOTS), col, ALU.mult, ALU.add))
            v.tensor_scalar(rel[:, :], rel[:, :], -2.0 * SLOTS, None, ALU.add).then_inc(rel_moved, 1)
            v.tensor_tensor(hot_col, row(iota[:, :], A), col.unsqueeze(2).to_broadcast([P, A, SLOTS]), ALU.is_equal)
            settled(v.tensor_tensor(hot_tile, row(iota[:, 0:TILES], A),
                                    tile_no.unsqueeze(2).to_broadcast([P, A, TILES]), ALU.is_equal))
            hot4 = hot_tile.rearrange("p (n k) c -> p n k c", k=2)
            val5 = slot_val.rearrange("p (n k) b c -> p n k b c", k=2)
            for k in range(2):
                v.tensor_tensor(val5[:, :, k, 0, :], hot4[:, :, k, :],
                                tokval[:, :].unsqueeze(2).to_broadcast([P, NT, TILES]), ALU.mult)
                last = v.tensor_tensor(val5[:, :, k, 1, :], hot4[:, :, k, :],
                                       gates[:, :, k].unsqueeze(2).to_broadcast([P, NT, TILES]), ALU.mult)
            last.then_inc(table_rhs_ready, 1)
            settled(v.tensor_tensor(over[0:1], upto[0:1].unsqueeze(1).to_broadcast([1, XTILES, E]),
                                    iota[0:1, 0:XTILES].unsqueeze(2).to_broadcast([1, XTILES, E]), ALU.is_le))
            settled(v.tensor_reduce(over_n[0:1], over[0:1], AX.X, ALU.add))
            v.tensor_scalar(extra[0:1, 0:XTILES], over_n[0:1], float(E - 1), None, ALU.min)
            v.tensor_copy(extra[0:1, XTILES:XTILES + 1], upto[0:1, E - 1:E]).then_inc(extra_ready, 1)
            dve.wait_ge(table_done, 1)
            token = ps[0:SLOTS, 7, 0:TILES]
            empty = past_cnt.rearrange("p e q -> p (e q)")[0:SLOTS, 0:TILES]
            v.tensor_copy(slot_gate[:, :], ps[:, 7, TILES:2 * TILES])
            settled(v.tensor_scalar(empty, token, 0.0, pad_row[0:SLOTS, :], ALU.is_equal, ALU.mult))
            settled(v.scalar_tensor_tensor(slot_row[0:SLOTS, :], token, -1.0, empty, ALU.add, ALU.add))
            dve.sem_inc(table_ready, 1)

            def products(seq):
                dve.wait_ge(silu_ready, seq + 1)
                dve.wait_ge(h_done, seq + 1)
                v.scalar_tensor_tensor(h_rows, silu, slot_gate[:, bass.DynSlice(seq, 1)], ps[:, B3, 0:FH],
                                       ALU.mult, ALU.mult).then_inc(h_ready, 1)

            def keep_hT(seq):
                dve.wait_ge(h_turned, seq + 1)
                v.tensor_copy(hT, ps[:, BHT, 0:2 * P].rearrange("p (c s) -> p c s", c=2)).then_inc(hT_ready, 1)

            def keep_y(u, seq, left):
                wait(dve, scattered, left * 16)
                dve.wait_ge(y_done, seq + 1)
                v.tensor_copy(ye[u][0:SLOTS, DH:D], ps[64:64 + SLOTS, BY, :]).then_inc(yhi_kept, 1)

            def tile(u, seq, left, hot_too=True):
                products(seq)
                if hot_too:
                    make_hot(seq + 2, (u + 2) % RING, seq)
                keep_hT(seq)
                keep_y(u, seq, left)

            for seq in range(RING):
                tile(seq, seq, 0)
            with dve.Fori(1, E // RING) as n:
                for u in range(RING):
                    tile(u, n * RING + u, n * RING + (u - 2))
            tile(0, E - 2, E - 4)
            tile(1, E - 1, E - 3, False)

            n_extra = dve.value_load(extra[0:1, XTILES:XTILES + 1], min_val=0, max_val=XTILES)
            with dve.If(n_extra > 0):
                with dve.Fori(0, n_extra) as i:
                    tile(2, i + E, i + E, False)
                    make_hot(i + E + 1, 2, i + E + 1)

            for j in range(NT):
                r, row_j = ROWS[j], total[0:ROWS[j], j, :]
                scale, bias = rstd[0:r, j, 0:1], rstd[0:r, j, 1:2]
                dve.wait_ge(total_loaded[j], 16)
                deviation_of(row_j, r)
                if j < SHARED:
                    scale_of(r, scale)
                    v.scalar_tensor_tensor(bias, mv[0:r, 0:1], -1.0, scale, ALU.mult, ALU.mult).then_inc(bias_ready, 1)
                else:
                    if j == SHARED:
                        dve.wait_ge(ln2_loaded, 32)
                    v.scalar_tensor_tensor(row_j, row_j, mv[0:r, 0:1], ln2[0:r, 0, :], ALU.subtract, ALU.mult)
                    scale_of(r, scale)
                    v.scalar_tensor_tensor(normed[0:r, j, :], row_j, scale, ln2[0:r, 1, :], ALU.mult,
                                           ALU.add).then_inc(dve_out, 1)


_INS = ["x_prompt", "x_sample", "state_pool", "state_conv", "w_in", "w_pool_map", "pool_scale", "conv_w", "w_out",
        "ln1_g", "ln1_b", "w_group", "b_group", "w_expert", "b_expert", "w1", "w3", "w2", "ln2_g", "ln2_b"]
_OUTS = [(1, SEQ, D), (NB, NS, D), (1, HIST, DP), (1, CHIST, DP), (NB, HIST, DP), (NB, CHIST, DP)]


def kernel(**inputs):
    import numpy as np
    import concourse.bacc as bacc
    from concourse.bass_utils import run_bass_kernel_spmd

    nc = bacc.Bacc("TRN2", target_bir_lowering=False, num_devices=1)
    arrays, args = {}, []
    for name in _INS:
        a = np.ascontiguousarray(inputs[name])
        arrays[f"in_{name}"] = a
        args.append(nc.dram_tensor(f"in_{name}", a.shape, mybir.dt.from_np(a.dtype), kind="ExternalInput").ap())
    for i, shape in enumerate(_OUTS):
        args.append(nc.dram_tensor(f"out_{i}", shape, F32, kind="ExternalOutput").ap())
    build(nc, *args)
    r = run_bass_kernel_spmd(nc, [arrays], core_ids=[0])
    return tuple(r.results[0][f"out_{i}"] for i in range(len(_OUTS)))
```
